# Optimizing a Trainium2 kernel written in Bass

```python
import math
import jax, jax.numpy as jnp
from jax import lax
import numpy as np

D_MODEL = 1024
BATCH = 1
SEQ = 512
DEPTH = 1

RET_HEADS = 4
RET_DV = D_MODEL // RET_HEADS
RET_DK = RET_DV // 2
RET_QK = RET_HEADS * RET_DK
RET_V = RET_HEADS * RET_DV
RET_CHUNK = 128
ROPE_BASE = 10000.0
CONV_WIDTH = D_MODEL
CONV_KERNEL = 31
PEER_HEADS = 8
PEER_DKEY = 256
PEER_NKEYS = 128
PEER_EXPERTS = PEER_NKEYS * PEER_NKEYS
PEER_TOPK = 16
PEER_BLOCK = 128
EPS = 1e-6
N_ADA = 6

kernel_name = "hybrid_retention_conformer_peer_block"

def _in_splits():
    widths = [RET_QK, RET_QK, RET_V, RET_V, CONV_WIDTH, CONV_WIDTH, D_MODEL, D_MODEL]
    return [int(s) for s in np.cumsum(widths)[:-1]]

def rms_norm(x, gain):
    xf = x.astype(jnp.float32)
    y = xf * lax.rsqrt(jnp.mean(xf * xf, axis=-1, keepdims=True) + EPS)
    return (y * gain.astype(jnp.float32)).astype(x.dtype)

def layer_norm(x, gain, bias):
    xf = x.astype(jnp.float32)
    mu = jnp.mean(xf, axis=-1, keepdims=True)
    var = jnp.mean(jnp.square(xf - mu), axis=-1, keepdims=True)
    y = (xf - mu) * lax.rsqrt(var + EPS)
    return (y * gain.astype(jnp.float32) + bias.astype(jnp.float32)).astype(x.dtype)

def rotary(t, positions):
    half = t.shape[-1] // 2
    inv_freq = ROPE_BASE ** (-jnp.arange(half, dtype=jnp.float32) / half)
    ang = positions.astype(jnp.float32)[:, :, None] * inv_freq
    cos = jnp.cos(ang)[:, :, None, :]
    sin = jnp.sin(ang)[:, :, None, :]
    t1 = t[..., :half].astype(jnp.float32)
    t2 = t[..., half:].astype(jnp.float32)
    out = jnp.concatenate([t1 * cos - t2 * sin, t1 * sin + t2 * cos], axis=-1)
    return out.astype(t.dtype)

def retention_chunkwise(q, k, v):
    B, S, H, dk = q.shape
    dv = v.shape[-1]
    C = RET_CHUNK
    n = S // C
    log_gamma = jnp.log1p(-jnp.exp2(-5.0 - jnp.arange(H, dtype=jnp.float32)))
    idx = jnp.arange(C, dtype=jnp.float32)
    diff = idx[:, None] - idx[None, :]
    decay_mask = jnp.where(diff[None] >= 0,
                           jnp.exp(jnp.maximum(diff, 0.0)[None] * log_gamma[:, None, None]),
                           0.0)
    zeta = jnp.exp((C - 1 - idx)[None, :] * log_gamma[:, None])
    xi = jnp.exp((idx + 1)[None, :] * log_gamma[:, None])
    chunk_decay = jnp.exp(C * log_gamma)

    def to_chunks(t):
        return t.reshape(B, n, C, H, t.shape[-1]).transpose(1, 0, 3, 2, 4)

    def step(state, chunk):
        qc, kc, vc = chunk
        scores = jnp.einsum('bhid,bhjd->bhij', qc, kc) * decay_mask[None]
        inner = jnp.einsum('bhij,bhje->bhie', scores, vc)
        cross = jnp.einsum('bhid,bhde->bhie', qc, state) * xi[None, :, :, None]
        new_state = state * chunk_decay[None, :, None, None] + jnp.einsum(
            'bhjd,bhje->bhde', kc * zeta[None, :, :, None], vc)
        return new_state, inner + cross

    state0 = jnp.zeros((B, H, dk, dv), jnp.float32)
    _, out = lax.scan(step, state0, (to_chunks(q), to_chunks(k), to_chunks(v)))
    return out.transpose(1, 0, 3, 2, 4).reshape(B, S, H, dv).astype(v.dtype)

def head_group_norm(y, gain):
    B, S, H, dv = y.shape
    yf = y.astype(jnp.float32)
    mu = jnp.mean(yf, axis=-1, keepdims=True)
    var = jnp.mean(jnp.square(yf - mu), axis=-1, keepdims=True)
    yn = ((yf - mu) * lax.rsqrt(var + EPS)).reshape(B, S, H * dv)
    return (yn * gain.astype(jnp.float32)).astype(y.dtype)

def hybrid_mixer(h, positions, w_in, ret_gn_gain, w_dw, b_dw, conv_ln_gain, conv_ln_bias,
                 w_pw2, w_out):
    B, S, _ = h.shape
    proj = h @ w_in
    q, k, v, g_ret, c_val, c_gate, gate_r, gate_c = jnp.split(proj, _in_splits(), axis=-1)
    q = rotary(q.reshape(B, S, RET_HEADS, RET_DK), positions)
    k = rotary(k.reshape(B, S, RET_HEADS, RET_DK), positions) * (RET_DK ** -0.5)
    v = v.reshape(B, S, RET_HEADS, RET_DV)
    ret = retention_chunkwise(q, k, v)
    ret = jax.nn.silu(g_ret) * head_group_norm(ret, ret_gn_gain)
    u = c_val * jax.nn.sigmoid(c_gate)
    u = lax.conv_general_dilated(u, w_dw, window_strides=(1,),
                                 padding=[(CONV_KERNEL - 1, 0)],
                                 dimension_numbers=('NWC', 'WIO', 'NWC'),
                                 feature_group_count=CONV_WIDTH) + b_dw
    conv = jax.nn.silu(layer_norm(u, conv_ln_gain, conv_ln_bias)) @ w_pw2
    merged = jax.nn.sigmoid(gate_r) * ret + jax.nn.sigmoid(gate_c) * conv
    return merged @ w_out

def peer_ffn(h, w_q, subkeys1, subkeys2, expert_u, expert_v):
    B, S, D = h.shape
    half = PEER_DKEY // 2
    blocks = h.reshape((B * S) // PEER_BLOCK, PEER_BLOCK, D)

    def block_fn(hb):
        qv = (hb @ w_q).reshape(PEER_BLOCK, PEER_HEADS, PEER_DKEY)
        s1 = jnp.einsum('thd,nd->thn', qv[..., :half], subkeys1)
        s2 = jnp.einsum('thd,nd->thn', qv[..., half:], subkeys2)
        v1, i1 = lax.top_k(s1, PEER_TOPK)
        v2, i2 = lax.top_k(s2, PEER_TOPK)
        cand_s = (v1[..., :, None] + v2[..., None, :]).reshape(PEER_BLOCK, PEER_HEADS, -1)
        cand_i = (i1[..., :, None] * PEER_NKEYS + i2[..., None, :]).reshape(PEER_BLOCK, PEER_HEADS, -1)
        top_s, pos = lax.top_k(cand_s, PEER_TOPK)
        eidx = jnp.take_along_axis(cand_i, pos, axis=-1)
        wts = jax.nn.softmax(top_s.astype(jnp.float32), axis=-1).astype(hb.dtype)
        ug = expert_u[eidx]
        act = jax.nn.gelu(jnp.einsum('thkd,td->thk', ug, hb))
        vg = expert_v[eidx]
        return jnp.einsum('thk,thkd->td', wts * act, vg)

    return lax.map(block_fn, blocks).reshape(B, S, D)

def setup_inputs(seed: int = 0) -> dict:
    key = jax.random.key(seed)
    ks = jax.random.split(key, 24)
    f32 = jnp.float32
    L = DEPTH
    n_in = 2 * RET_QK + 2 * RET_V + 2 * CONV_WIDTH + 2 * D_MODEL

    def nrm(k, shape, scale):
        return jax.random.normal(k, shape, f32) * scale

    def gain(k, shape):
        return 1.0 + 0.02 * jax.random.normal(k, shape, f32)

    x = jax.random.normal(ks[0], (BATCH, SEQ, D_MODEL), f32)
    c = jax.random.normal(ks[1], (BATCH, D_MODEL), f32)
    offsets = jax.random.randint(ks[2], (BATCH, 1), 0, 4096, dtype=jnp.int32)
    positions = (offsets + jnp.arange(SEQ, dtype=jnp.int32)[None, :]).astype(jnp.int32)
    return {
        "x": x,
        "c": c,
        "positions": positions,
        "w_ada": nrm(ks[3], (L, D_MODEL, N_ADA * D_MODEL), 0.5 * D_MODEL ** -0.5),
        "b_ada": nrm(ks[4], (L, N_ADA * D_MODEL), 0.01),
        "norm_mix_gain": gain(ks[5], (L, D_MODEL)),
        "w_in": nrm(ks[6], (L, D_MODEL, n_in), D_MODEL ** -0.5),
        "ret_gn_gain": gain(ks[7], (L, RET_V)),
        "w_dw": nrm(ks[8], (L, CONV_KERNEL, 1, CONV_WIDTH), CONV_KERNEL ** -0.5),
        "b_dw": nrm(ks[9], (L, CONV_WIDTH), 0.01),
        "conv_ln_gain": gain(ks[10], (L, CONV_WIDTH)),
        "conv_ln_bias": nrm(ks[11], (L, CONV_WIDTH), 0.01),
        "w_pw2": nrm(ks[12], (L, CONV_WIDTH, D_MODEL), CONV_WIDTH ** -0.5),
        "w_out": nrm(ks[13], (L, D_MODEL, D_MODEL), D_MODEL ** -0.5),
        "norm_ffn_gain": gain(ks[14], (L, D_MODEL)),
        "w_peer_q": nrm(ks[15], (L, D_MODEL, PEER_HEADS * PEER_DKEY), D_MODEL ** -0.5),
        "peer_subkeys1": nrm(ks[16], (L, PEER_NKEYS, PEER_DKEY // 2), (PEER_DKEY // 2) ** -0.5),
        "peer_subkeys2": nrm(ks[17], (L, PEER_NKEYS, PEER_DKEY // 2), (PEER_DKEY // 2) ** -0.5),
        "peer_u": nrm(ks[18], (L, PEER_EXPERTS, D_MODEL), D_MODEL ** -0.5),
        "peer_v": nrm(ks[19], (L, PEER_EXPERTS, D_MODEL), PEER_TOPK ** -0.5),
        "final_norm_gain": gain(ks[20], (D_MODEL,)),
    }

def reference(x, c, positions, w_ada, b_ada, norm_mix_gain, w_in, ret_gn_gain, w_dw, b_dw,
              conv_ln_gain, conv_ln_bias, w_pw2, w_out, norm_ffn_gain, w_peer_q,
              peer_subkeys1, peer_subkeys2, peer_u, peer_v, final_norm_gain):
    cond = jax.nn.silu(c)
    for l in range(DEPTH):
        ada = cond @ w_ada[l] + b_ada[l]
        sh1, sc1, g1, sh2, sc2, g2 = jnp.split(ada[:, None, :], N_ADA, axis=-1)
        h = rms_norm(x, norm_mix_gain[l]) * (1.0 + sc1) + sh1
        x = x + g1 * hybrid_mixer(h, positions, w_in[l], ret_gn_gain[l], w_dw[l], b_dw[l],
                                  conv_ln_gain[l], conv_ln_bias[l], w_pw2[l], w_out[l])
        h = rms_norm(x, norm_ffn_gain[l]) * (1.0 + sc2) + sh2
        x = x + g2 * peer_ffn(h, w_peer_q[l], peer_subkeys1[l], peer_subkeys2[l],
                              peer_u[l], peer_v[l])
    return rms_norm(x, final_norm_gain)


_drawn_inputs = setup_inputs


def setup_inputs(seed=0):
    import zlib

    import numpy as np

    out = dict(_drawn_inputs(seed))
    spreads = {}
    factors = {'b_ada': 6.718,
     'norm_mix_gain': 8.0,
     'ret_gn_gain': 22.319,
     'b_dw': 64.0,
     'conv_ln_gain': 64.0,
     'conv_ln_bias': 200.0,
     'norm_ffn_gain': 63.156,
     'final_norm_gain': 27.342}
    for name, (base, spread) in spreads.items():
        noise = np.random.default_rng([zlib.crc32(name.encode()), seed]).standard_normal(out[name].shape)
        drawn = base * np.exp(spread * noise) if base else spread * noise
        out[name] = __import__('jax').numpy.asarray(drawn.astype(out[name].dtype))
    for name, factor in factors.items():
        out[name] = (out[name] * factor).astype(out[name].dtype)
    return out
```

```python
from contextlib import ExitStack

import numpy as np

import concourse.bass as bass
from concourse import mybir

ALU = mybir.AluOpType
ACT = mybir.ActivationFunctionType
F32 = mybir.dt.float32
F32R = mybir.dt.float32r
U32 = mybir.dt.uint32
I32 = mybir.dt.int32
AX_X = mybir.AxisListType.X

P = 128
KB = 1024
EPS = 1e-6
ROPE_BASE = 10000.0
RET_HEADS = 4
PEER_HEADS = 8
TOPK = 16
TURN_1 = 6.28125
TURN_2 = 0.00193500518798828125
TURN_3 = float(2 * np.pi - TURN_1 - TURN_2)
ROUND_MAGIC = float(3 << 22)
SIN_LIMIT = 3.1415925
VERY_LOW = -3.0e38


def shape_tables():
    h = np.arange(RET_HEADS, dtype=np.float64)
    log_gamma = np.log1p(-np.exp2(-5.0 - h))
    j, i = np.arange(P)[:, None], np.arange(P)[None, :]
    full = np.exp((i - j)[:, None, :] * log_gamma[None, :, None]) * P ** -0.5
    causal = np.where((i >= j)[:, None, :], full, 0.0)
    inv_freq = ROPE_BASE ** (-np.arange(P // 2) / (P // 2))
    cols = [causal.reshape(P, -1), full.reshape(P, -1), np.eye(P),
            np.tile(inv_freq, (P, 1)), np.tile(np.arange(TOPK), (P, 1))]
    return np.concatenate(cols, axis=1).astype(np.float32)


def wait_apart(eng, sem, count, holding):
    count = count if isinstance(count, int) else eng.to_reg(count)
    eng.wait_ge(holding, 1)
    eng.wait_ge(sem, count)


class Steps:

    def __init__(self, eng, sem):
        self.eng, self.sem, self.n, self.var, self.per = eng, sem, 0, None, 0

    def inc(self, instruction):
        instruction.then_inc(self.sem, 1)
        self.n += 1

    def wait(self):
        self.eng.wait_ge(self.sem, self.n if self.var is None else self.var * self.per + self.n)

    def wait_apart(self):
        if self.var is None:
            self.wait()
        else:
            wait_apart(self.eng, self.sem, self.var * self.per + self.n, self.sem)

    def do(self, instruction):
        self.inc(instruction)
        self.wait()

    def loop(self, var, per):
        self.var, self.per, self.start = var, per, self.n

    def end(self, rounds):
        assert self.n == self.start + self.per, (self.n - self.start, self.per)
        self.n, self.var = self.start + self.per * rounds, None


def block_program(nc, x, c, positions, w_ada, b_ada, norm_mix_gain, w_in, ret_gn_gain, w_dw, b_dw,
                  conv_ln_gain, conv_ln_bias, w_pw2, w_out, norm_ffn_gain, w_peer_q, peer_subkeys1,
                  peer_subkeys2, peer_u, peer_v, final_norm_gain, tables, out):
    T, D = x.shape[1], x.shape[2]
    NB = T // P
    KD = D // P
    HU = KD // 2
    NC = 512
    TAPS = w_dw.shape[1]
    PAD = TAPS - 1
    NKEYS, DHALF = peer_subkeys1.shape[1], peer_subkeys1.shape[2]
    DKEY = 2 * DHALF
    DV = D // RET_HEADS
    QKV = 2 * RET_HEADS * P
    PAIRS = NB * TOPK
    NG = 8
    assert NB == 4 and KD == 8 and DHALF == P and NKEYS == P and DV == 2 * P and 2 * PAIRS % NG == 0

    with ExitStack() as ctx:
        def sem(name):
            return ctx.enter_context(nc.semaphore(name))

        def at(name, shape, offset, dt=F32):
            return nc.alloc_sbuf_tensor_at(name, shape, dt, offset=16 * KB + 512 + offset)[:]

        R = [i * 16 * KB for i in range(7)] + [113 * KB, 129 * KB]
        W = 145 * KB
        hT_hi, hT_lo = at("hT_hi", [P, KD, T], R[0], F32R), at("hT_lo", [P, KD, T], R[1], F32R)
        sub_raw = at("sub_raw", [P, 2, P], R[1])
        qk_rot = at("qk_rot", [P, NB, QKV], R[0])
        ret_scores = at("ret_scores", [P, NB, T], R[0])
        cv_v, cv_s, cv_y, cv_t = (at(f"cv_{n}", [P, T], R[0] + (8 + 2 * i) * KB) for i, n in enumerate("vsyt"))
        qT, kT = at("qT", [P, RET_HEADS, T], R[1]), at("kT", [P, RET_HEADS, T], R[1] + 8 * KB)
        ada_acc2 = at("ada_acc2", [P, 4 * D], R[2])
        qk_raw = at("qk_raw", [P, NB, QKV], R[2])
        x1 = at("x1", [P, NB, D], R[2])
        ada_w = at("ada_w", [P, 2, 2 * D], R[3])
        val = at("val", [P, NB, D], R[3])
        h2 = at("h2", [P, NB, D], R[3])
        shift1, scale1 = at("shift1", [P, D], R[4]), at("scale1", [P, D], R[4] + 4 * KB)
        ret_gate = at("ret_gate", [P, NB, D], R[4])
        x_in = at("x_in", [P, NB, D], R[5])
        gate_tmp = at("gate_tmp", [P, NB, NC], R[5])
        conv_gate = at("conv_gate", [P, NB, D], R[5])
        gathered = at("gathered", [P, NG, D], R[4])
        glu = at("glu", [P, KD, PAD + T], R[6])
        squares = at("squares", [P, 2, T], R[6])
        ang, cos_, rest, sin_ = (at(n, [P, NB, P // 2], R[6] + (4 + i) * KB)
                                 for i, n in enumerate(("ang", "cos_", "rest", "sin_")))
        rot_tmp = at("rot_tmp", [P, 2, QKV // 2], R[6] + 8 * KB)
        retn = at("retn", [P, NB, D], R[6])
        conv = at("conv", [P, KD, T], R[7])
        yacc = at("yacc", [P, NB, D], R[7])
        ada_acc1 = at("ada_acc1", [P, 2 * D], R[7])
        junk = at("junk", [P, D], R[7] + 8 * KB)
        cols = at("cols", [P, D], R[7] + 12 * KB)
        mod = at("mod", [P, 4, D], R[8])
        GATE1, SHIFT2, SCALE2, GATE2 = range(4)
        w_raw = at("w_raw", [P, 2, HU, NC], W)
        w_hi = at("w_hi", [P, 2, HU, NC], W + 16 * KB, F32R)
        w_lo = at("w_lo", [P, 2, HU, NC], W + 32 * KB, F32R)
        wq_raw = at("wq_raw", [P, KD, DKEY], W)
        wq_hi = at("wq_hi", [P, KD, DKEY], W + 16 * KB, F32R)
        wq_lo = at("wq_lo", [P, KD, DKEY], W + 24 * KB, F32R)
        queryT = at("queryT", [P, 2, T], W + 32 * KB)
        scores = at("scores", [P, 2, NB, NKEYS], W + 36 * KB)
        cand = at("cand", [P, TOPK * TOPK], W + 40 * KB)
        onehot = at("onehot", [P, 2, TOPK, TOPK], W + 41 * KB)

        def placer(start, end):
            state = [start]

            def place(name, shape, dt=F32):
                t = at(name, shape, state[0], dt)
                state[0] += (int(np.prod(shape[1:])) * 4 + 31) // 32 * 32
                assert state[0] <= end, (name, state[0])
                return t
            return place

        place = placer(W + 48 * KB, 229344 - 16 * KB - 512)
        row = place("row", [P, D])
        NT = 2 * RET_HEADS * P + P + P // 2 + TOPK
        tab = place("tab", [P, NT])
        ones = place("ones", [P, P])
        colsT = place("colsT", [P, KD, TAPS + 3])
        skT = place("skT", [P, 2, NKEYS])
        cond = place("cond", [P, KD])
        pos_i = place("pos_i", [P, NB], I32)
        pos_f = place("pos_f", [P, NB])
        NS = NB * RET_HEADS
        stat = place("stat", [P, NS, 6])
        mv = place("mv", [P, NS, 2])
        n_v, n_s, n_y, n_t = (place(f"n_{n}", [P, NS]) for n in "vsyt")
        place = placer(W + 43 * KB, W + 48 * KB)
        vals = place("vals", [P, 2, TOPK])
        idx_u = place("idx_u", [P, 2, TOPK], U32)
        idx_f = place("idx_f", [P, 2, TOPK])
        top = place("top", [P, NB, TOPK])
        neg_max = place("neg_max", [P, NB])
        pos_u = place("pos_u", [P, TOPK], U32)
        pick_u = place("pick_u", [P, 2, TOPK], U32)
        pick_f = place("pick_f", [P, 2, TOPK])
        found = place("found", [P, 2, TOPK])
        expert_next = place("expert_next", [P, PAIRS], U32)
        expert_u = place("expert_u", [P, PAIRS], U32)
        expert_v = place("expert_v", [P, PAIRS], U32)
        exp_next = place("exp_next", [P, NB, TOPK])
        exp_now = place("exp_now", [P, NB, TOPK])
        sum_next = place("sum_next", [P, NB])
        rsum_now = place("rsum_now", [P, NB])
        dots = place("dots", [P, NB, TOPK])
        gelu = place("gelu", [P, NB, TOPK])
        coef = place("coef", [P, NB, TOPK])

        HP = RET_HEADS * P
        causal = tab[:, 0:HP].rearrange("p (h i) -> p h i", h=RET_HEADS)
        decay = tab[:, HP:2 * HP].rearrange("p (h i) -> p h i", h=RET_HEADS)
        ident = tab[:, 2 * HP:2 * HP + P]
        inv_freq = tab[:, 2 * HP + P:NT - TOPK]
        iota = tab[:, NT - TOPK:NT]
        ps = ctx.enter_context(nc.psum_tensor("ps", [P, 8, NC], F32))

        tab_in, c_in, x_loaded, b_ada_in, pos_in = (sem(n) for n in ("tab_in", "c_in", "x_loaded", "b_ada_in", "pos_in"))
        cols_in, sub_in, row_in, x_again = (sem(n) for n in ("cols_in", "sub_in", "row_in", "x_again"))
        ada_in = [sem("ada_in0"), sem("ada_in1")]
        w_loaded = [sem("w_loaded0"), sem("w_loaded1")]
        wq_loaded = sem("wq_loaded")
        g_loaded = [sem(f"g_loaded{i}") for i in range(NG)]
        zeroed, silu_c, ada_used = sem("zeroed"), sem("silu_c"), sem("ada_used")
        w_high, w_low, half_done = sem("w_high"), sem("w_low"), sem("half_done")
        bank_ready = sem("bank_ready")
        bank_free = [sem(f"bank_free{i}") for i in range(4)]
        job_ready = sem("job_ready")
        job_free = [sem(f"job_free{i}") for i in range(4)]
        dve_steps, conv_steps = sem("dve_steps"), sem("conv_steps")
        sumsq, var_ready, std_ready = sem("sumsq"), sem("var_ready"), sem("std_ready")
        tokens_ready, high_ready = sem("tokens_ready"), sem("high_ready")
        gate_written, gain_applied, row_used = sem("gate_written"), sem("gain_applied"), sem("row_used")
        glu_zero, angles, sines, rotated = sem("glu_zero"), sem("angles"), sem("sines"), sem("rotated")
        conv_done, centered, squared, y_ready, y_silu, y_high, y_low = (
            sem(n) for n in ("conv_done", "centered", "squared", "y_ready", "y_silu", "y_high", "y_low"))
        merged, x1_ready = sem("merged"), sem("x1_ready")
        wq_high, wq_low = sem("wq_high"), sem("wq_low")
        topk_done, top_ready, exp_ready = sem("topk_done"), sem("top_ready"), sem("exp_ready")
        idx_copied, dots_done, gelu_done = sem("idx_copied"), sem("dots_done"), sem("gelu_done")
        g_free = [sem(f"g_free{i}") for i in range(NG)]
        out_ready, out_written = sem("out_ready"), sem("out_written")

        jobs = [("cols", 0), ("cols", 1), ("sub", 0)]
        jobs += [("hT", i) for i in range(2 * NB)] + [("ada", i) for i in range(2 * NB)]
        jobs += [("rot", i) for i in range(2 * NB)] + [("mean", 0), ("var", 0)]
        for h in range(RET_HEADS):
            jobs += [("scores", h, j) for j in range(NB)] + [("ret", h, g) for g in range(NB // 2)]
        jobs += [("mT", i) for i in range(2 * NB)] + [("h2T", i) for i in range(2 * NB)]
        JOB = {name: n for n, name in enumerate(jobs)}

        def job_bank(*job):
            return ps[:, 4 + JOB[job] % 4, :]

        def job_may_start(pe, *job):
            if JOB[job] >= 4:
                pe.wait_ge(job_free[JOB[job] % 4], JOB[job] // 4)

        def job_is_ready(eng, *job):
            eng.wait_ge(job_ready, JOB[job] + 1)

        def job_freed(*job):
            return job_free[JOB[job] % 4]

        def job_is_read(eng, *job):
            eng.wait_ge(job_free[JOB[job] % 4], JOB[job] // 4 + 1)

        GLU_COL = QKV + 2 * D
        N_GLU, N_TOK = 2 * D // NC, (w_in.shape[2] - 2 * D) // NC
        N_LOW = GLU_COL // NC
        PW = 1 + N_GLU + N_TOK
        WO = PW + D // NC
        N_CH = WO + D // NC
        GATE_R = 1 + N_GLU + N_LOW
        GATE_C = GATE_R + D // NC
        w_in_v, w_pw_v, w_out_v, w_q_v = (w[0].rearrange("(k p) n -> p k n", p=P)
                                          for w in (w_in, w_pw2, w_out, w_peer_q))
        w_ada_v = w_ada[0].rearrange("(p j) n -> p j n", j=KD)

        def bank_is_read(eng, ch, i):
            eng.wait_ge(bank_free[i], ch + 1)

        block = ctx.enter_context(nc.Block())

        @block.sync
        def _(sp):
            def weight_unit(view, col, unit, half, first=False):
                if not first:
                    sp.wait_ge(w_low, unit - 1)
                sp.dma_start(w_raw[:, half], view[:, HU * half:HU * half + HU, bass.ds(col, NC)]).then_inc(w_loaded[half], 16)

            def ada_unit(a):
                part, j = divmod(a, KD)
                if a >= 2:
                    sp.wait_ge(ada_used, a - 1)
                sp.dma_start(ada_w[:, a % 2], w_ada_v[:, j, part * 2 * D:(part + 1) * 2 * D]).then_inc(ada_in[a % 2], 16)

            sp.dma_start(cond, c.rearrange("a (p j) -> p (a j)", j=KD)).then_inc(c_in, 16)
            for a in range(KD):
                ada_unit(a)
            for ch in range(N_GLU):
                for half in range(2):
                    u = 2 * ch + half
                    weight_unit(w_in_v, GLU_COL + ch * NC, u, half, first=u < 2)
                    ada_unit(KD + 2 * u)
                    ada_unit(KD + 2 * u + 1)
            with sp.Fori(0, N_LOW) as ch:
                for half in range(2):
                    weight_unit(w_in_v, ch * NC, ch * 2 + (2 * N_GLU + half), half)
            with sp.Fori(0, N_TOK - N_LOW) as ch:
                for half in range(2):
                    weight_unit(w_in_v, ch * NC + (GLU_COL + 2 * D), ch * 2 + (2 * (N_GLU + N_LOW) + half), half)
            for n, view in enumerate((w_pw_v, w_out_v)):
                for ch in range(D // NC):
                    for half in range(2):
                        weight_unit(view, ch * NC, 2 * (N_GLU + N_TOK + 2 * n + ch) + half, half)
                if n == 0:
                    sp.wait_ge(rotated, NB)
                    sp.dma_start(x1, x[0].rearrange("(b p) d -> p b d", p=P)).then_inc(x_again, 16)
            sp.wait_ge(w_low, 2 * (N_CH - 1))
            sp.dma_start(wq_raw, w_q_v[:, :, 0:DKEY]).then_inc(wq_loaded, 16)
            with sp.Fori(1, PEER_HEADS) as h:
                sp.wait_ge(wq_low, h)
                sp.dma_start(wq_raw, w_q_v[:, :, bass.ds(h * DKEY, DKEY)]).then_inc(wq_loaded, 16)
            out_v = out[0].rearrange("(b p) d -> p b d", p=P)
            for b in range(NB):
                sp.wait_ge(out_ready, b + 1)
                sp.dma_start(out_v[:, b], yacc[:, b]).then_inc(out_written, 16)
            sp.wait_ge(out_written, 16 * NB)

        @block.gpsimd
        def _(pool):
            pool.memset(ada_acc1, 0.0).then_inc(zeroed, 1)
            pool.memset(ada_acc2, 0.0).then_inc(zeroed, 1)
            pool.memset(cols, 0.0).then_inc(zeroed, 1)
            pool.memset(ones, 1.0).then_inc(zeroed, 1)
            pool.memset(glu[:, :, 0:PAD], 0.0).then_inc(glu_zero, 1)

            def low_part(u, half):
                pool.wait_ge(w_high, u + 1)
                pool.tensor_tensor(w_lo[:, half], w_raw[:, half], w_hi[:, half].bitcast(F32),
                                   ALU.subtract).then_inc(w_low, 1)

            low_part(0, 0)
            low_part(1, 1)
            with pool.Fori(1, GATE_R) as ch:
                for half in range(2):
                    low_part(ch * 2 + half, half)
            for ch in range(GATE_R, N_CH):
                if ch < N_CH - 1:
                    low_part(2 * ch, 0)
                if ch < GATE_C:
                    for b in range(NB):
                        n = (ch - GATE_R) * NB + b
                        pool.wait_ge(gate_written, n + 1)
                        g = ret_gate[:, b, bass.ds((ch - GATE_R) * NC, NC)]
                        pool.tensor_tensor(g, g, gate_tmp[:, b], ALU.mult).then_inc(bank_free[b], 1)
                if ch < N_CH - 1:
                    low_part(2 * ch + 1, 1)
                if ch == GATE_C:
                    pool.wait_ge(row_in, 32)
                    for b in range(NB):
                        bank_is_read(pool, GATE_C - 1, b)
                        pool.tensor_tensor(ret_gate[:, b], ret_gate[:, b], row, ALU.mult).then_inc(gain_applied, 1)

            def query_low(h):
                pool.wait_ge(wq_high, h + 1)
                pool.tensor_tensor(wq_lo, wq_raw, wq_hi.bitcast(F32), ALU.subtract).then_inc(wq_low, 1)

            def head(h, query, following):
                for n in range(2 * PAIRS):
                    if n == PAIRS:
                        if query:
                            query_low(h + 2)
                        wait_apart(pool, dots_done, h * NB + 1, topk_done)
                        pool.tensor_copy(expert_v, expert_u).then_inc(idx_copied, 1)
                        pool.wait_ge(idx_copied, h * 2 + 2)
                    wait_apart(pool, g_free[n % NG], h * (2 * PAIRS // NG) + (n // NG + 1), topk_done)
                    if n < PAIRS:
                        table, idx = peer_u[0], expert_u[:, n:n + 1]
                    else:
                        k, b = divmod(n - PAIRS, NB)
                        table, idx = peer_v[0], expert_v[:, b * TOPK + k:b * TOPK + k + 1]
                    pool.indirect_dma_start(out=gathered[:, n % NG], out_offset=None, in_=table,
                                            in_offset=bass.IndirectOffsetOnAxis(ap=idx, axis=0)
                                            ).then_inc(g_loaded[n % NG], 16)
                if following:
                    next_indices(h + 1)

            def next_indices(h):
                if not isinstance(h, int) or h:
                    pool.wait_ge(dots_done, h * NB)
                wait_apart(pool, topk_done, h * NB + NB, topk_done)
                pool.tensor_copy(expert_u, expert_next).then_inc(idx_copied, 1)
                pool.wait_ge(idx_copied, h * 2 + 1)

            query_low(0)
            query_low(1)
            next_indices(0)
            with pool.Fori(0, PEER_HEADS - 2) as h:
                head(h, True, True)
            head(PEER_HEADS - 2, False, True)
            head(PEER_HEADS - 1, False, False)

        @block.scalar
        def _(act):
            act.dma_start(tab, tables).then_inc(tab_in, 16)
            act.dma_start(x_in, x[0].rearrange("(b p) d -> p b d", p=P)).then_inc(x_loaded, 16)
            act.dma_start(row, norm_mix_gain[0].partition_broadcast(P)).then_inc(row_in, 16)
            act.dma_start(sub_raw[:, 0], peer_subkeys1[0]).then_inc(sub_in, 16)
            act.dma_start(sub_raw[:, 1], peer_subkeys2[0]).then_inc(sub_in, 16)
            act.dma_start(pos_i, positions[0].rearrange("(b p) -> p b", p=P),
                          allow_slow_non_contiguous=True).then_inc(pos_in, 16)
            act.wait_ge(zeroed, 3)
            act.dma_start(ada_acc1[0:1, :], b_ada[:, 0:2 * D]).then_inc(b_ada_in, 16)
            act.dma_start(ada_acc2[0:1, :], b_ada[:, 2 * D:6 * D]).then_inc(b_ada_in, 16)
            act.dma_start(cols[0:TAPS, :], w_dw[0, :, 0, :]).then_inc(cols_in, 16)
            for n, v in enumerate((b_dw, conv_ln_gain, conv_ln_bias)):
                act.dma_start(cols[TAPS + n:TAPS + n + 1, :], v).then_inc(cols_in, 16)
            act.wait_ge(c_in, 16)
            act.activation(cond, cond, ACT.Silu).then_inc(silu_c, 1)
            act.wait_ge(x_loaded, 16)
            for b in range(NB):
                if b:
                    act.wait_ge(sumsq, b)
                act.activation(junk, x_in[:, b], ACT.Square, accum_out=n_s[:, b:b + 1]).then_inc(sumsq, 1)
            for i in range(2):
                job_is_ready(act, "cols", i)
                act.activation(colsT[:, 4 * i:4 * i + 4, :],
                               job_bank("cols", i).rearrange("p (a b) -> p a b", a=4)[:, :, 0:TAPS + 3],
                               ACT.Copy).then_inc(job_freed("cols", i), 1)
            job_is_ready(act, "sub", 0)
            act.activation(skT.rearrange("p a b -> p (a b)"), job_bank("sub", 0)[:, 0:2 * P],
                           ACT.Copy).then_inc(job_freed("sub", 0), 1)

            def square_root(n, dst, src):
                act.wait_ge(var_ready, n)
                act.activation(dst, src, ACT.Sqrt).then_inc(std_ready, 1)

            square_root(1, n_s[:, 0:NB], n_v[:, 0:NB])
            for i in range(2):
                act.wait_ge(bank_ready, i + 1)
                act.activation(shift1[:, i * NC:(i + 1) * NC], ps[:, i], ACT.Copy).then_inc(bank_free[i], 1)

            def transposed_high(kind, dst):
                for n in range(2 * NB):
                    b, half = divmod(n, 2)
                    job_is_ready(act, kind, n)
                    act.activation(dst[:, HU * half:HU * half + HU, b * P:(b + 1) * P],
                                   job_bank(kind, n).rearrange("p (a b) -> p a b", a=HU),
                                   ACT.Copy).then_inc(high_ready, 1)

            def weight_high(ch, half):
                act.wait_ge(w_loaded[half], 16 * ch)
                if ch > 1 and half == 0:
                    act.wait_ge(half_done, ch - 1)
                if ch > 1 and half == 1:
                    act.wait_ge(bank_ready, 4 * ch)
                act.activation(w_hi[:, half], w_raw[:, half], ACT.Copy).then_inc(w_high, 1)

            transposed_high("hT", hT_hi)
            weight_high(1, 0)
            weight_high(1, 1)
            for ch in range(1, PW):
                weight_high(ch + 1, 0)
                k = ch - 1 - N_GLU
                for i in range(4):
                    func, half = ACT.Copy, slice(k % 2 * NC, k % 2 * NC + NC)
                    if ch <= N_GLU // 2:
                        dst = glu[:, 4 * (ch - 1) + i, PAD:PAD + T]
                        act.wait_ge(glu_zero, 1)
                    elif ch <= N_GLU:
                        dst, func = conv[:, 4 * (ch - 1 - N_GLU // 2) + i], ACT.Sigmoid
                    elif k < 2:
                        dst = qk_raw[:, i, half]
                    elif k < 4:
                        dst = val[:, i, half]
                    elif k < 6:
                        dst, func = ret_gate[:, i, half], ACT.Silu
                    elif ch < GATE_C:
                        dst, func = gate_tmp[:, i], ACT.Sigmoid
                    else:
                        dst, func = conv_gate[:, i, half], ACT.Sigmoid
                    act.wait_ge(bank_ready, 4 * ch + i + 1)
                    branch = GATE_R <= ch < GATE_C
                    if branch and ch > GATE_R:
                        bank_is_read(act, ch - 1, i)
                    act.activation(dst, ps[:, i], func).then_inc(gate_written if branch else bank_free[i], 1)
                weight_high(ch + 1, 1)
                if ch == N_GLU:
                    for i in range(2 * NB):
                        job_is_ready(act, "ada", i)
                        act.activation(mod[:, i // 2, i % 2 * NC:i % 2 * NC + NC], job_bank("ada", i),
                                       ACT.Copy).then_inc(job_freed("ada", i), 1)
                    act.wait_ge(row_used, 1)
                    act.dma_start(row, ret_gn_gain[0].partition_broadcast(P)).then_inc(row_in, 16)
            act.wait_ge(angles, 2)
            act.activation(sin_, ang, ACT.Sin).then_inc(sines, 1)
            act.activation(cos_, rest, ACT.Sin).then_inc(sines, 1)
            for n in range(2 * NB):
                b, half = divmod(n, 2)
                job_is_ready(act, "rot", n)
                act.activation((kT if half else qT)[:, :, b * P:(b + 1) * P],
                               job_bank("rot", n).rearrange("p (a b) -> p a b", a=RET_HEADS),
                               ACT.Copy).then_inc(job_freed("rot", n), 1)
            for t in range(KD):
                act.wait_ge(centered, t + 1)
                if t >= 2:
                    act.wait_ge(conv_done, t - 1)
                act.activation(squares[:, t % 2], conv[:, t], ACT.Square).then_inc(squared, 1)
            square_root(2, cv_s, cv_v)
            job_is_ready(act, "var", 0)
            for h in range(RET_HEADS):
                for g in range(NB // 2):
                    job_is_ready(act, "ret", h, g)
                    act.activation(retn[:, 2 * g:2 * g + 2, h * DV:(h + 1) * DV],
                                   job_bank("ret", h, g).rearrange("p (a b) -> p a b", a=2),
                                   ACT.Copy).then_inc(job_freed("ret", h, g), 1)
            for t in range(KD):
                act.wait_ge(y_ready, t + 1)
                act.activation(conv[:, t], conv[:, t], ACT.Silu, bias=colsT[:, t, TAPS + 2:TAPS + 3],
                               scale=colsT[:, t, TAPS + 1:TAPS + 2]).then_inc(y_silu, 1)
                act.wait_ge(y_silu, t + 1)
                act.activation(hT_hi[:, t], conv[:, t], ACT.Copy).then_inc(y_high, 1)
            square_root(3, n_s, n_v)
            weight_high(PW + 1, 0)
            weight_high(PW + 1, 1)
            act.wait_ge(gain_applied, NB)
            act.dma_start(row, norm_ffn_gain[0].partition_broadcast(P)).then_inc(row_in, 16)
            weight_high(WO, 0)
            weight_high(WO, 1)
            transposed_high("mT", hT_hi)
            weight_high(WO + 1, 0)
            weight_high(WO + 1, 1)
            for b in range(NB):
                act.wait_ge(x1_ready, (D // NC - 1) * NB + b + 1)
                act.activation(retn[:, b], x1[:, b], ACT.Square, accum_out=n_s[:, b:b + 1]).then_inc(sumsq, 1)
            square_root(4, n_s[:, 0:NB], n_v[:, 0:NB])
            act.wait_ge(row_used, 2)
            act.dma_start(row, final_norm_gain.partition_broadcast(P)).then_inc(row_in, 16)
            transposed_high("h2T", hT_hi)

            def query_high(h, first=False):
                act.wait_ge(wq_loaded, h * 16 + 16)
                if not first:
                    act.wait_ge(bank_ready, h * 4 + (4 * N_CH - 2))
                act.activation(wq_hi, wq_raw, ACT.Copy).then_inc(wq_high, 1)

            def query_copy(h):
                for half in range(2):
                    act.wait_ge(bank_ready, h * 4 + (4 * N_CH + half + 1))
                    act.activation(queryT[:, half], ps[:, half], ACT.Copy).then_inc(bank_free[half], 1)

            def score_copy(h, first=False):
                for half in range(2):
                    act.wait_ge(bank_ready, h * 4 + (4 * N_CH + half + 3))
                    if not first:
                        act.wait_ge(topk_done, h * NB)
                    act.activation(scores[:, half].rearrange("p b n -> p (b n)"), ps[:, 2 + half],
                                   ACT.Copy).then_inc(bank_free[2 + half], 1)

            def exponentials(h):
                for b in range(NB):
                    act.wait_ge(top_ready, h * NB + (b + 1))
                    act.activation(exp_next[:, b], top[:, b], ACT.Exp, bias=neg_max[:, b:b + 1],
                                   accum_out=sum_next[:, b:b + 1]).then_inc(exp_ready, 1)

            def gelus(h):
                for b in range(NB):
                    act.wait_ge(dots_done, h * NB + (b + 1))
                    act.activation(gelu[:, b], dots[:, b], ACT.Gelu_apprx_tanh).then_inc(gelu_done, 1)

            act.wait_ge(bank_ready, 4 * N_CH)
            query_high(0, first=True)
            query_copy(0)
            score_copy(0, first=True)
            query_high(1)
            query_copy(1)
            exponentials(0)
            score_copy(1)
            with act.Fori(0, PEER_HEADS - 2) as h:
                query_high(h + 2)
                query_copy(h + 2)
                exponentials(h + 1)
                score_copy(h + 2)
                gelus(h)
            exponentials(PEER_HEADS - 1)
            gelus(PEER_HEADS - 2)
            gelus(PEER_HEADS - 1)
            for b in range(NB):
                act.wait_ge(x1_ready, D // NC * NB + b + 1)
                act.activation(retn[:, b], x1[:, b], ACT.Square, accum_out=n_s[:, b:b + 1]).then_inc(sumsq, 1)
            square_root(5, n_s[:, 0:NB], n_v[:, 0:NB])

        @block.tensor
        def _(pe):
            def product3(dst, stat_, moving, start, stop):
                (sh, sl), (mh, ml) = stat_, moving
                pe.matmul(dst, sh, mh, start=start, stop=False)
                pe.matmul(dst, sh, ml, start=False, stop=False)
                return pe.matmul(dst, sl, mh, start=False, stop=stop)

            def both(hi, lo, *index):
                return hi[index], lo[index]

            def chunk(ch, tokens_stationary):
                for half in range(2):
                    pe.wait_ge(w_low, ch * 2 + (half - 1))
                    for i in range(4):
                        if half == 0:
                            pe.wait_ge(bank_free[i], ch)
                        for k in range(HU):
                            tok = (slice(None), HU * half + k, slice(i * P, (i + 1) * P) if tokens_stationary else slice(None))
                            w = (slice(None), half, k, slice(None) if tokens_stationary else slice(i * P, (i + 1) * P))
                            tok, w = both(hT_hi, hT_lo, *tok), both(w_hi, w_lo, *w)
                            a, b = (tok, w) if tokens_stationary else (w, tok)
                            mm = product3(ps[:, i], a, b, half == 0 and k == 0, half == 1 and k == HU - 1)
                        if half == 1:
                            mm.then_inc(bank_ready, 1)
                    if half == 0:
                        mm.then_inc(half_done, 1)

            def transposes(job, sources):
                job_may_start(pe, *job)
                for n, src in enumerate(sources):
                    mm = pe.transpose(job_bank(*job)[:, n * P:(n + 1) * P], src, ident)
                mm.then_inc(job_ready, 1)

            def token_transposes(kind, src, ready):
                for n in range(2 * NB):
                    b, half = divmod(n, 2)
                    ready(b, half)
                    transposes((kind, n), [src[:, b, (HU * half + k) * P:(HU * half + k + 1) * P] for k in range(HU)])

            pe.wait_ge(tab_in, 16)
            pe.wait_ge(zeroed, 4)
            pe.wait_ge(cols_in, 64)
            for i in range(2):
                transposes(("cols", i), [cols[:, (4 * i + k) * P:(4 * i + k + 1) * P] for k in range(4)])
            pe.wait_ge(sub_in, 32)
            transposes(("sub", 0), [sub_raw[:, 0], sub_raw[:, 1]])
            pe.wait_ge(ada_used, KD)
            for i in range(4):
                pe.matmul(ps[:, i], ones, ada_acc1[:, i * NC:(i + 1) * NC], start=True, stop=True).then_inc(bank_ready, 1)
            token_transposes("hT", x_in, lambda b, half: pe.wait_ge(tokens_ready, b + 1))
            job_is_read(pe, "hT", 6)
            job_is_read(pe, "hT", 7)
            with pe.Fori(1, 1 + N_GLU) as ch:
                chunk(ch, False)
            pe.wait_ge(ada_used, 3 * KD)
            for i in range(2 * NB):
                job_may_start(pe, "ada", i)
                pe.matmul(job_bank("ada", i), ones, ada_acc2[:, i * NC:(i + 1) * NC],
                          start=True, stop=True).then_inc(job_ready, 1)
            with pe.Fori(1 + N_GLU, PW) as ch:
                chunk(ch, True)
            for n in range(2 * NB):
                b, half = divmod(n, 2)
                pe.wait_ge(rotated, b + 1)
                transposes(("rot", n), [qk_rot[:, b, (RET_HEADS * half + h) * P:(RET_HEADS * half + h + 1) * P]
                                        for h in range(RET_HEADS)])
            job_may_start(pe, "mean", 0)
            pe.wait_ge(conv_steps, KD * TAPS)
            for t in range(KD):
                mm = pe.matmul(job_bank("mean", 0), ones, conv[:, t], start=t == 0, stop=t == KD - 1)
            mm.then_inc(job_ready, 1)
            job_may_start(pe, "var", 0)
            for t in range(KD):
                pe.wait_ge(squared, t + 1)
                mm = pe.matmul(job_bank("var", 0), ones, squares[:, t % 2], start=t == 0, stop=t == KD - 1)
                mm.then_inc(conv_done if t < KD - 1 else job_ready, 1)
            for n in range(2 * NB):
                job_is_read(pe, "rot", n)
            for h in range(RET_HEADS):
                for j in range(NB):
                    job_may_start(pe, "scores", h, j)
                    pe.matmul(job_bank("scores", h, j)[:, j * P:T], kT[:, h, j * P:(j + 1) * P], qT[:, h, j * P:T],
                              start=True, stop=True).then_inc(job_ready, 1)
                for g in range(NB // 2):
                    job_may_start(pe, "ret", h, g)
                    for j in range(2 * g + 2):
                        if 2 * g <= j or g == 0:
                            job_is_read(pe, "scores", h, j)
                    for bb in range(2):
                        b = 2 * g + bb
                        for j in range(b + 1):
                            mm = pe.matmul(job_bank("ret", h, g)[:, bb * DV:(bb + 1) * DV],
                                           ret_scores[:, j, b * P:(b + 1) * P], val[:, j, h * DV:(h + 1) * DV],
                                           start=j == 0, stop=j == b)
                    mm.then_inc(job_ready, 1)
            pe.wait_ge(y_low, KD)
            for ch in range(PW, WO):
                chunk(ch, True)
            token_transposes("mT", conv_gate, lambda b, half: pe.wait_ge(merged, half * NB + b + 1))
            job_is_read(pe, "mT", 6)
            job_is_read(pe, "mT", 7)
            for ch in range(WO, N_CH):
                chunk(ch, True)
            token_transposes("h2T", h2, lambda b, half: pe.wait_ge(tokens_ready, NB + b + 1))
            job_is_read(pe, "h2T", 6)
            job_is_read(pe, "h2T", 7)
            with pe.Fori(0, PEER_HEADS) as h:
                pe.wait_ge(wq_low, h + 1)
                for half in range(2):
                    pe.wait_ge(bank_free[half], h + N_CH)
                    for k in range(KD):
                        mm = product3(ps[:, half],
                                      both(wq_hi, wq_lo, slice(None), k, slice(half * DHALF, (half + 1) * DHALF)),
                                      both(hT_hi, hT_lo, slice(None), k, slice(None)), k == 0, k == KD - 1)
                    mm.then_inc(bank_ready, 1)
                for half in range(2):
                    pe.wait_ge(bank_free[half], h + (N_CH + 1))
                    pe.wait_ge(bank_free[2 + half], h + N_CH)
                    for b in range(NB):
                        mm = pe.matmul(ps[:, 2 + half, b * NKEYS:(b + 1) * NKEYS], queryT[:, half, b * P:(b + 1) * P],
                                       skT[:, half], start=True, stop=True)
                    mm.then_inc(bank_ready, 1)

        @block.vector
        def _(dve):
            st = Steps(dve, dve_steps)

            def root_reciprocal(n, v, s, y, t):
                dve.wait_ge(std_ready, n)
                st.do(dve.reciprocal(y, s))
                st.do(dve.tensor_tensor(t, v, y, ALU.mult))
                st.do(dve.tensor_tensor(t, t, y, ALU.mult))
                st.do(dve.tensor_scalar(t, t, -0.5, 1.5, ALU.mult, ALU.add))
                st.do(dve.tensor_tensor(y, y, t, ALU.mult))

            def token_variance(n):
                dve.wait_ge(sumsq, n * NB)
                dve.tensor_scalar(n_v[:, 0:NB], n_s[:, 0:NB], 1.0 / D, EPS, ALU.mult, ALU.add).then_inc(var_ready, 1)
                dve.wait_ge(var_ready, {1: 1, 2: 4, 3: 5}[n])

            def transposed_low(kind, dst_hi, dst_lo, before):
                for n in range(2 * NB):
                    b, half = divmod(n, 2)
                    dve.wait_ge(high_ready, before + n + 1)
                    part = (slice(None), slice(HU * half, HU * half + HU), slice(b * P, (b + 1) * P))
                    dve.tensor_tensor(dst_lo[part], job_bank(kind, n).rearrange("p (a b) -> p a b", a=HU),
                                      dst_hi[part].bitcast(F32), ALU.subtract).then_inc(job_freed(kind, n), 1)

            dve.wait_ge(silu_c, 1)
            dve.wait_ge(b_ada_in, 32)

            def ada_sum(a, acc):
                j = a % KD
                dve.wait_ge(ada_in[a % 2], 16 * (a // 2 + 1))
                dve.scalar_tensor_tensor(out=acc, in0=ada_w[:, a % 2], scalar=cond[:, j:j + 1], in1=acc,
                                         op0=ALU.mult, op1=ALU.add).then_inc(ada_used, 1)
                dve.wait_ge(ada_used, a + 1)

            for a in range(KD):
                ada_sum(a, ada_acc1)
            token_variance(1)
            root_reciprocal(1, n_v[:, 0:NB], n_s[:, 0:NB], n_y[:, 0:NB], n_t[:, 0:NB])
            dve.wait_ge(row_in, 16)
            for i in range(2):
                dve.wait_ge(bank_ready, 2 + i + 1)
                cols_i = slice(i * NC, (i + 1) * NC)
                dve.scalar_tensor_tensor(out=scale1[:, cols_i], in0=ps[:, 2 + i], scalar=1.0, in1=row[:, cols_i],
                                         op0=ALU.add, op1=ALU.mult).then_inc(bank_free[2 + i], 1)
                bank_is_read(dve, 0, i)
                bank_is_read(dve, 0, 2 + i)
            for b in range(NB):
                st.do(dve.scalar_tensor_tensor(out=x_in[:, b], in0=x_in[:, b], scalar=n_y[:, b:b + 1], in1=scale1,
                                               op0=ALU.mult, op1=ALU.mult))
                if b == 0:
                    dve.engine_nop().then_inc(row_used, 1)
                dve.tensor_tensor(x_in[:, b], x_in[:, b], shift1, ALU.add).then_inc(tokens_ready, 1)
            transposed_low("hT", hT_hi, hT_lo, 0)
            for a in range(KD, 3 * KD):
                ada_sum(a, ada_acc2[:, (a // KD - 1) * 2 * D:(a // KD) * 2 * D])

            for i in range(4):
                bank_is_read(dve, N_GLU, i)
            st.do(dve.tensor_tensor(glu[:, :, PAD:PAD + T], glu[:, :, PAD:PAD + T], conv, ALU.mult))
            job_is_read(dve, "cols", 0)
            job_is_read(dve, "cols", 1)
            for t in range(KD):
                dve.tensor_scalar(conv[:, t], glu[:, t, 0:T], colsT[:, t, 0:1], colsT[:, t, TAPS:TAPS + 1],
                                  ALU.mult, ALU.add).then_inc(conv_steps, 1)
            with dve.Fori(1, TAPS) as tap:
                for t in range(KD):
                    dve.wait_ge(conv_steps, tap * KD + (t + 1 - KD))
                    dve.scalar_tensor_tensor(out=conv[:, t], in0=glu[:, t, bass.ds(tap, T)],
                                             scalar=colsT[:, t, bass.ds(tap, 1)], in1=conv[:, t],
                                             op0=ALU.mult, op1=ALU.add).then_inc(conv_steps, 1)
            dve.wait_ge(conv_steps, KD * TAPS)

            dve.wait_ge(pos_in, 16)
            st.do(dve.tensor_copy(pos_f, pos_i))
            for b in range(NB):
                st.inc(dve.tensor_scalar(ang[:, b], inv_freq, pos_f[:, b:b + 1], None, ALU.mult))
            st.wait()
            st.do(dve.tensor_scalar(rest, ang, float(1 / (2 * np.pi)), ROUND_MAGIC, ALU.mult, ALU.add))
            st.do(dve.tensor_scalar(rest, rest, ROUND_MAGIC, None, ALU.subtract))
            for part in (TURN_1, TURN_2, TURN_3):
                st.do(dve.scalar_tensor_tensor(out=ang, in0=rest, scalar=-part, in1=ang, op0=ALU.mult, op1=ALU.add))
            dve.tensor_scalar(ang, ang, SIN_LIMIT, -SIN_LIMIT, ALU.min, ALU.max).then_inc(angles, 1)
            dve.wait_ge(angles, 1)
            st.do(dve.scalar_tensor_tensor(out=rest, in0=ang, scalar=-1.0, in1=ang, op0=ALU.mult, op1=ALU.max))
            dve.tensor_scalar(rest, rest, -1.0, float(np.pi / 2), ALU.mult, ALU.add).then_inc(angles, 1)
            dve.wait_ge(sines, 2)
            for i in range(4):
                bank_is_read(dve, 2 + N_GLU, i)
            for b in range(NB):
                raw = qk_raw[:, b].rearrange("p (h s d) -> p h s d", s=2, d=P // 2)
                rot = qk_rot[:, b].rearrange("p (h s d) -> p h s d", s=2, d=P // 2)
                first, second = raw[:, :, 0], raw[:, :, 1]
                cos_b, sin_b = (v[:, b].unsqueeze(1).broadcast_to([P, 2 * RET_HEADS, P // 2]) for v in (cos_, sin_))
                t0, t1 = (rot_tmp[:, i].rearrange("p (h d) -> p h d", d=P // 2) for i in range(2))
                st.inc(dve.tensor_tensor(rot[:, :, 0], first, cos_b, ALU.mult))
                st.inc(dve.tensor_tensor(t0, second, sin_b, ALU.mult))
                st.inc(dve.tensor_tensor(rot[:, :, 1], first, sin_b, ALU.mult))
                st.inc(dve.tensor_tensor(t1, second, cos_b, ALU.mult))
                st.wait()
                st.inc(dve.tensor_tensor(rot[:, :, 0], rot[:, :, 0], t0, ALU.subtract))
                st.wait()
                dve.tensor_tensor(rot[:, :, 1], rot[:, :, 1], t1, ALU.add).then_inc(rotated, 1)
                dve.wait_ge(rotated, b + 1)

            job_is_ready(dve, "mean", 0)
            for t in range(KD):
                ins = dve.scalar_tensor_tensor(out=conv[:, t], in0=job_bank("mean", 0), scalar=-1.0 / D, in1=conv[:, t],
                                               op0=ALU.mult, op1=ALU.add)
                ins.then_inc(centered if t < KD - 1 else job_freed("mean", 0), 1)
            job_is_read(dve, "mean", 0)
            dve.engine_nop().then_inc(centered, 1)
            job_is_ready(dve, "var", 0)
            dve.tensor_scalar(cv_v, job_bank("var", 0), 1.0 / D, EPS, ALU.mult, ALU.add).then_inc(job_freed("var", 0), 1)
            job_is_read(dve, "var", 0)
            dve.engine_nop().then_inc(var_ready, 1)
            root_reciprocal(2, cv_v, cv_s, cv_y, cv_t)
            for t in range(KD):
                dve.tensor_tensor(conv[:, t], conv[:, t], cv_y, ALU.mult).then_inc(y_ready, 1)

            for h in range(RET_HEADS):
                gamma = 1.0 - 2.0 ** (-5.0 - h)
                for j in range(NB):
                    job_is_ready(dve, "scores", h, j)
                    if h and j == 0:
                        job_is_read(dve, "ret", h - 1, 0)
                        job_is_read(dve, "ret", h - 1, 1)
                    bank = job_bank("scores", h, j)
                    for i in range(j, NB):
                        blk = slice(i * P, (i + 1) * P)
                        if i == j:
                            ins = dve.tensor_tensor(ret_scores[:, j, blk], bank[:, blk], causal[:, h], ALU.mult)
                        else:
                            ins = dve.scalar_tensor_tensor(out=ret_scores[:, j, blk], in0=bank[:, blk],
                                                           scalar=float(gamma ** (P * (i - j))), in1=decay[:, h],
                                                           op0=ALU.mult, op1=ALU.mult)
                    ins.then_inc(job_freed("scores", h, j), 1)
            for n in range(NS):
                b, h = divmod(n, RET_HEADS)
                job_is_read(dve, "ret", h, b // 2)
                st.inc(dve.bn_stats(stat[:, n], retn[:, b, h * DV:(h + 1) * DV]))
            st.wait()
            for n in range(NS):
                st.inc(dve.bn_aggr(mv[:, n], stat[:, n]))
            st.wait()
            dve.tensor_scalar(n_v, mv[:, :, 1], EPS, None, ALU.add).then_inc(var_ready, 1)
            dve.wait_ge(var_ready, 3)
            for t in range(KD):
                dve.wait_ge(y_high, t + 1)
                dve.tensor_tensor(hT_lo[:, t], conv[:, t], hT_hi[:, t].bitcast(F32), ALU.subtract).then_inc(y_low, 1)
            root_reciprocal(3, n_v, n_s, n_y, n_t)
            for n in range(NS):
                b, h = divmod(n, RET_HEADS)
                part = retn[:, b, h * DV:(h + 1) * DV]
                st.inc(dve.tensor_scalar(part, part, mv[:, n, 0:1], n_y[:, n:n + 1], ALU.subtract, ALU.mult))
            st.wait()
            dve.wait_ge(gain_applied, NB)
            for b in range(NB):
                st.inc(dve.tensor_tensor(retn[:, b], retn[:, b], ret_gate[:, b], ALU.mult))
            for i in range(2 * NB):
                job_is_read(dve, "ada", i)
            dve.wait_ge(row_in, 48)
            dve.scalar_tensor_tensor(out=mod[:, SCALE2], in0=mod[:, SCALE2], scalar=1.0, in1=row,
                                     op0=ALU.add, op1=ALU.mult).then_inc(row_used, 1)
            st.wait()
            for ch in range(PW, WO):
                for b in range(NB):
                    part = (slice(None), b, slice((ch - PW) * NC, (ch - PW + 1) * NC))
                    dve.wait_ge(bank_ready, 4 * ch + b + 1)
                    dve.tensor_tensor(conv_gate[part], ps[:, b], conv_gate[part], ALU.mult).then_inc(bank_free[b], 1)
                    bank_is_read(dve, ch, b)
                    dve.tensor_tensor(conv_gate[part], conv_gate[part], retn[part], ALU.add).then_inc(merged, 1)
            transposed_low("mT", hT_hi, hT_lo, 2 * NB)
            dve.wait_ge(x_again, 16)
            for ch in range(WO, N_CH):
                for b in range(NB):
                    half = slice((ch - WO) * NC, (ch - WO + 1) * NC)
                    dve.wait_ge(bank_ready, 4 * ch + b + 1)
                    dve.tensor_tensor(retn[:, b, half], ps[:, b], mod[:, GATE1, half], ALU.mult).then_inc(bank_free[b], 1)
                    bank_is_read(dve, ch, b)
                    dve.tensor_tensor(x1[:, b, half], x1[:, b, half], retn[:, b, half], ALU.add).then_inc(x1_ready, 1)
            token_variance(2)
            root_reciprocal(4, n_v[:, 0:NB], n_s[:, 0:NB], n_y[:, 0:NB], n_t[:, 0:NB])
            dve.wait_ge(row_used, 2)
            for b in range(NB):
                st.do(dve.scalar_tensor_tensor(out=h2[:, b], in0=x1[:, b], scalar=n_y[:, b:b + 1], in1=mod[:, SCALE2],
                                               op0=ALU.mult, op1=ALU.mult))
                dve.tensor_tensor(h2[:, b], h2[:, b], mod[:, SHIFT2], ALU.add).then_inc(tokens_ready, 1)
            dve.wait_ge(tokens_ready, 2 * NB)
            transposed_low("h2T", hT_hi, hT_lo, 4 * NB)
            for s in range(NG):
                dve.memset(yacc.rearrange("p b d -> p (b d)")[:, s * NB * D // NG:(s + 1) * NB * D // NG],
                           0.0).then_inc(g_free[s], 1)

            def topk(h, b):
                if b == 0:
                    for half in range(2):
                        wait_apart(dve, bank_free[2 + half], h + (N_CH + 1), sumsq)
                for half in range(2):
                    st.inc(dve.max(vals[:, half, 0:8], scores[:, half, b]))
                st.wait_apart()
                for half in range(2):
                    st.inc(dve.max_index(idx_u[:, half, 0:8], vals[:, half, 0:8], scores[:, half, b]))
                    st.inc(dve.match_replace(scores[:, half, b], vals[:, half, 0:8], scores[:, half, b], VERY_LOW))
                st.wait_apart()
                for half in range(2):
                    st.inc(dve.max(vals[:, half, 8:16], scores[:, half, b]))
                st.wait_apart()
                for half in range(2):
                    st.inc(dve.max_index(idx_u[:, half, 8:16], vals[:, half, 8:16], scores[:, half, b]))
                grid = [P, TOPK, TOPK]
                st.wait()
                st.inc(dve.tensor_tensor(cand.rearrange("p (i j) -> p i j", i=TOPK),
                                        vals[:, 0].unsqueeze(2).broadcast_to(grid),
                                        vals[:, 1].unsqueeze(1).broadcast_to(grid), ALU.add))
                st.wait_apart()
                st.inc(dve.max(top[:, b, 0:8], cand))
                st.wait_apart()
                st.inc(dve.max_index(pos_u[:, 0:8], top[:, b, 0:8], cand))
                st.inc(dve.match_replace(cand, top[:, b, 0:8], cand, VERY_LOW))
                st.wait_apart()
                st.inc(dve.max(top[:, b, 8:16], cand))
                st.wait_apart()
                st.inc(dve.max_index(pos_u[:, 8:16], top[:, b, 8:16], cand))
                dve.tensor_scalar(neg_max[:, b:b + 1], top[:, b, 0:1], -1.0, None, ALU.mult).then_inc(top_ready, 1)
                st.inc(dve.tensor_copy(idx_f, idx_u))
                st.wait()
                st.inc(dve.tensor_scalar(pick_u[:, 0], pos_u, 4, None, ALU.logical_shift_right))
                st.do(dve.tensor_scalar(pick_u[:, 1], pos_u, TOPK - 1, None, ALU.bitwise_and))
                st.do(dve.tensor_copy(pick_f, pick_u))
                for half in range(2):
                    st.inc(dve.tensor_tensor(onehot[:, half], iota.unsqueeze(1).broadcast_to(grid),
                                             pick_f[:, half].unsqueeze(2).broadcast_to(grid), ALU.is_equal))
                st.wait()
                for half in range(2):
                    st.inc(dve.tensor_tensor(onehot[:, half], onehot[:, half],
                                             idx_f[:, half].unsqueeze(1).broadcast_to(grid), ALU.mult))
                st.wait()
                st.do(dve.tensor_reduce(found.rearrange("p a b -> p (a b)"),
                                        onehot.rearrange("p a k i -> p (a k) i"), AX_X, ALU.add))
                dve.scalar_tensor_tensor(out=expert_next[:, b * TOPK:(b + 1) * TOPK], in0=found[:, 0],
                                         scalar=float(NKEYS), in1=found[:, 1], op0=ALU.mult,
                                         op1=ALU.add).then_inc(topk_done, 1)

            USES = 2 * PAIRS // NG

            def rows_are_loaded(h, n):
                dve.wait_ge(g_loaded[n % NG], h * (16 * USES) + 16 * (n // NG + 1))

            def head(h, following):
                dve.wait_ge(exp_ready, h * NB + NB)
                st.inc(dve.tensor_copy(exp_now, exp_next))
                st.inc(dve.reciprocal(rsum_now, sum_next))
                for b in range(NB):
                    for k in range(TOPK):
                        n = b * TOPK + k
                        rows_are_loaded(h, n)
                        g = gathered[:, n % NG]
                        dve.tensor_tensor_reduce(g, g, h2[:, b], 1.0, 0.0, ALU.mult, ALU.add,
                                                 dots[:, b, k:k + 1]).then_inc(g_free[n % NG], 1)
                    for s in range(NG):
                        wait_apart(dve, g_free[s], h * USES + (1 + (b + 1) * TOPK // NG), sumsq)
                    dve.engine_nop().then_inc(dots_done, 1)
                    if following:
                        topk(h + 1, b)
                for b in range(NB):
                    dve.wait_ge(gelu_done, h * NB + (b + 1))
                    st.inc(dve.scalar_tensor_tensor(out=coef[:, b], in0=gelu[:, b], scalar=rsum_now[:, b:b + 1],
                                                    in1=exp_now[:, b], op0=ALU.mult, op1=ALU.mult))
                st.wait()
                for m in range(PAIRS):
                    k, b = divmod(m, NB)
                    n = PAIRS + m
                    rows_are_loaded(h, n)
                    if m >= NB:
                        dve.wait_ge(g_free[(n - NB) % NG], h * USES + ((n - NB) // NG + 2))
                    dve.scalar_tensor_tensor(out=yacc[:, b], in0=gathered[:, n % NG], scalar=coef[:, b, k:k + 1],
                                             in1=yacc[:, b], op0=ALU.mult, op1=ALU.add).then_inc(g_free[n % NG], 1)

            before = st.n
            for b in range(NB):
                topk(0, b)
            per_topk = st.n - before
            with dve.Fori(0, PEER_HEADS - 1) as h:
                st.loop(h, per_topk + 2 + NB)
                head(h, True)
            st.end(PEER_HEADS - 1)
            head(PEER_HEADS - 1, False)
            for s in range(NG):
                dve.wait_ge(g_free[s], PEER_HEADS * USES + 1)

            for b in range(NB):
                st.inc(dve.tensor_tensor(yacc[:, b], yacc[:, b], mod[:, GATE2], ALU.mult))
            st.wait()
            for b in range(NB):
                dve.tensor_tensor(x1[:, b], x1[:, b], yacc[:, b], ALU.add).then_inc(x1_ready, 1)
            token_variance(3)
            root_reciprocal(5, n_v[:, 0:NB], n_s[:, 0:NB], n_y[:, 0:NB], n_t[:, 0:NB])
            dve.wait_ge(row_in, 64)
            for b in range(NB):
                dve.scalar_tensor_tensor(out=yacc[:, b], in0=x1[:, b], scalar=n_y[:, b:b + 1], in1=row,
                                         op0=ALU.mult, op1=ALU.mult).then_inc(out_ready, 1)


_INS = ["x", "c", "positions", "w_ada", "b_ada", "norm_mix_gain", "w_in", "ret_gn_gain", "w_dw", "b_dw",
        "conv_ln_gain", "conv_ln_bias", "w_pw2", "w_out", "norm_ffn_gain", "w_peer_q", "peer_subkeys1",
        "peer_subkeys2", "peer_u", "peer_v", "final_norm_gain"]


def kernel(**inputs):
    import concourse.bacc as bacc
    from concourse.bass_utils import run_bass_kernel_spmd

    nc = bacc.Bacc("TRN2", target_bir_lowering=False, num_devices=1)
    arrays = {name: np.ascontiguousarray(inputs[name]) for name in _INS}
    arrays["tables"] = shape_tables()
    args = {name: nc.dram_tensor(f"in_{name}", a.shape, mybir.dt.from_np(a.dtype), kind="ExternalInput").ap()
            for name, a in arrays.items()}
    out = nc.dram_tensor("out_block", arrays["x"].shape, F32, kind="ExternalOutput").ap()
    block_program(nc, **args, out=out)
    r = run_bass_kernel_spmd(nc, [{f"in_{name}": a for name, a in arrays.items()}], core_ids=[0])
    return r.results[0]["out_block"]
```

```python
from contextlib import ExitStack

import numpy as np

import concourse.bass as bass
from concourse import mybir

ALU = mybir.AluOpType
ACT = mybir.ActivationFunctionType
F32 = mybir.dt.float32
F32R = mybir.dt.float32r
U32 = mybir.dt.uint32
I32 = mybir.dt.int32
AX_X = mybir.AxisListType.X

P = 128
KB = 1024
EPS = 1e-6
ROPE_BASE = 10000.0
RET_HEADS = 4
PEER_HEADS = 8
TOPK = 16
TURN_1 = 6.28125
TURN_2 = 0.00193500518798828125
TURN_3 = float(2 * np.pi - TURN_1 - TURN_2)
ROUND_MAGIC = float(3 << 22)
SIN_LIMIT = 3.1415925
VERY_LOW = -3.0e38


def shape_tables():
    h = np.arange(RET_HEADS, dtype=np.float64)
    log_gamma = np.log1p(-np.exp2(-5.0 - h))
    j, i = np.arange(P)[:, None], np.arange(P)[None, :]
    full = np.exp((i - j)[:, None, :] * log_gamma[None, :, None]) * P ** -0.5
    causal = np.where((i >= j)[:, None, :], full, 0.0)
    inv_freq = ROPE_BASE ** (-np.arange(P // 2) / (P // 2))
    cols = [causal.reshape(P, -1), full.reshape(P, -1), np.eye(P),
            np.tile(inv_freq, (P, 1)), np.tile(np.arange(P), (P, 1))]
    return np.concatenate(cols, axis=1).astype(np.float32)


def wait_apart(eng, sem, count, holding):
    count = count if isinstance(count, int) else eng.to_reg(count)
    eng.wait_ge(holding, 1)
    eng.wait_ge(sem, count)


class Steps:

    def __init__(self, eng, sem):
        self.eng, self.sem, self.n, self.var, self.per = eng, sem, 0, None, 0

    def inc(self, instruction):
        instruction.then_inc(self.sem, 1)
        self.n += 1

    def wait(self):
        self.eng.wait_ge(self.sem, self.n if self.var is None else self.var * self.per + self.n)

    def wait_apart(self):
        if self.var is None:
            self.wait()
        else:
            wait_apart(self.eng, self.sem, self.var * self.per + self.n, self.sem)

    def do(self, instruction):
        self.inc(instruction)
        self.wait()

    def loop(self, var, per):
        self.var, self.per, self.start = var, per, self.n

    def end(self, rounds):
        assert self.n == self.start + self.per, (self.n - self.start, self.per)
        self.n, self.var = self.start + self.per * rounds, None


def block_program(nc, x, c, positions, w_ada, b_ada, norm_mix_gain, w_in, ret_gn_gain, w_dw, b_dw,
                  conv_ln_gain, conv_ln_bias, w_pw2, w_out, norm_ffn_gain, w_peer_q, peer_subkeys1,
                  peer_subkeys2, peer_u, peer_uT, peer_v, final_norm_gain, tables, out):
    T, D = x.shape[1], x.shape[2]
    NB = T // P
    KD = D // P
    HU = KD // 2
    NC = 512
    TAPS = w_dw.shape[1]
    PAD = TAPS - 1
    NKEYS, DHALF = peer_subkeys1.shape[1], peer_subkeys1.shape[2]
    DKEY = 2 * DHALF
    DV = D // RET_HEADS
    QKV = 2 * RET_HEADS * P
    TILES = peer_uT.shape[0]
    ND = NB - 1
    TD = ND * P
    GT = 8
    GROUPS = TD // GT
    GB = P // GT
    TB = 24
    PIECES = 8
    RAW = 4
    W_TILE = 40
    NPAIR = PEER_HEADS * TOPK
    NG = 3
    G_BODY = NPAIR // NG
    G_REST = NPAIR - NG * G_BODY
    assert NB == 4 and KD == 8 and DHALF == P and NKEYS == P and DV == 2 * P and PEER_HEADS * TOPK == P and TILES == NKEYS

    with ExitStack() as ctx:
        def sem(name):
            return ctx.enter_context(nc.semaphore(name))

        def at(name, shape, offset, dt=F32):
            return nc.alloc_sbuf_tensor_at(name, shape, dt, offset=16 * KB + 512 + offset)[:]

        R = [i * 16 * KB for i in range(7)] + [113 * KB, 129 * KB]
        W = 145 * KB
        hT_hi, hT_lo = at("hT_hi", [P, KD, T], R[0], F32R), at("hT_lo", [P, KD, T], R[1], F32R)
        sub_raw = at("sub_raw", [P, 2, P], R[1])
        qk_rot = at("qk_rot", [P, NB, QKV], R[0])
        ret_scores = at("ret_scores", [P, NB, T], R[0])
        cv_v, cv_s, cv_y, cv_t = (at(f"cv_{n}", [P, T], R[0] + (8 + 2 * i) * KB) for i, n in enumerate("vsyt"))
        qT, kT = at("qT", [P, RET_HEADS, T], R[1]), at("kT", [P, RET_HEADS, T], R[1] + 8 * KB)
        ada_acc2 = at("ada_acc2", [P, 4 * D], R[2])
        qk_raw = at("qk_raw", [P, NB, QKV], R[2])
        x1 = at("x1", [P, NB, D], R[2])
        ada_w = at("ada_w", [P, 2, 2 * D], R[3])
        val = at("val", [P, NB, D], R[3])
        h2 = at("h2", [P, NB, D], R[3])
        shift1, scale1 = at("shift1", [P, D], R[4]), at("scale1", [P, D], R[4] + 4 * KB)
        ret_gate = at("ret_gate", [P, NB, D], R[4])
        x_in = at("x_in", [P, NB, D], R[5])
        gate_tmp = at("gate_tmp", [P, NB, NC], R[5])
        conv_gate = at("conv_gate", [P, NB, D], R[5])
        glu = at("glu", [P, KD, PAD + T], R[6])
        squares = at("squares", [P, 2, T], R[6])
        ang, cos_, rest, sin_ = (at(n, [P, NB, P // 2], R[6] + (4 + i) * KB)
                                 for i, n in enumerate(("ang", "cos_", "rest", "sin_")))
        rot_tmp = at("rot_tmp", [P, 2, QKV // 2], R[6] + 8 * KB)
        retn = at("retn", [P, NB, D], R[6])
        conv = at("conv", [P, KD, T], R[7])
        ada_acc1 = at("ada_acc1", [P, 2 * D], R[7])
        junk = at("junk", [P, D], R[7] + 8 * KB)
        cols = at("cols", [P, D], R[7] + 12 * KB)
        mod = at("mod", [P, 4, D], R[8])
        GATE1, SHIFT2, SCALE2, GATE2 = range(4)
        w_raw = at("w_raw", [P, 2, HU, NC], W)
        w_hi = at("w_hi", [P, 2, HU, NC], W + 16 * KB, F32R)
        w_lo = at("w_lo", [P, 2, HU, NC], W + 32 * KB, F32R)
        tile_raw = [at(f"tile_raw{n}", [P, KD, P], R[3] + 4 * n * KB) for n in range(2)]
        tile_raw += [at(f"tile_raw{n}", [P, KD, T], R[n - 2])[:, :, TD:T] for n in range(2, RAW)]

        def by_k(tile):
            return tile.rearrange("p (k e) -> p k e", k=KD)

        yacc = at("yacc", [P, D], R[3] + 8 * KB)
        tile_hi = at("tile_hi", [P, 2, D], W + 32 * KB, F32R)
        gathered = [at(f"gathered{n}", [P, D], o) for n, o in enumerate((W + 28 * KB, W + 40 * KB, W + 44 * KB))]
        scores = at("scores", [P, 2 * PEER_HEADS, T], R[4])
        stage = at("stage", [P, NKEYS, P], R[4])
        acts_in, routes_in = (at(n, [P, RAW, TD], R[4] + 6 * i * KB) for i, n in enumerate(("acts_in", "routes_in")))
        weighted = at("weighted", [P, 2, TD], R[4] + 12 * KB)
        wt_hi, wt_lo = (at(n, [P, 2, TD], R[4] + (16 + 4 * i) * KB, F32R) for i, n in enumerate(("wt_hi", "wt_lo")))
        out_buf = at("out_buf", [P, NB, D], R[4] + 24 * KB)
        pairs = at("pairs", [P, 3, NB, P], R[8])
        pairsT = at("pairsT", [P, 3, TD], R[8] + 6 * KB)
        K1, K2, WT = range(3)
        dots = at("dots", [P, NPAIR], R[8] + 11 * KB)
        dots_now = at("dots_now", [P, NG], R[8] + 11 * KB + 512)
        queryT = at("queryT", [P, 4, T], R[6] + 16 * KB)
        hot = at("hot", [P, 2, GT, 2, P], W)
        tile_lo = at("tile_lo", [P, 2, D], W + 16 * KB, F32R)
        acts = at("acts", [P, 2, TD], W + 24 * KB)
        squares_out = at("squares_out", [P, NB, D], R[0])
        work = at("work", [P, 2, NB, NKEYS], R[6])
        cand = at("cand", [P, NB, TOPK * TOPK], R[6] + 4 * KB)
        onehot = at("onehot", [P, 2, NB * TOPK, TOPK], R[6] + 8 * KB)

        def placer(start, end):
            state = [start]

            def place(name, shape, dt=F32):
                t = at(name, shape, state[0], dt)
                state[0] += (int(np.prod(shape[1:])) * 4 + 31) // 32 * 32
                assert state[0] <= end, (name, state[0])
                return t
            return place

        place = placer(W + 48 * KB, 229344 - 16 * KB - 512)
        row = place("row", [P, D])
        NT = 2 * RET_HEADS * P + P + P // 2 + P
        tab = place("tab", [P, NT])
        ones = place("ones", [P, P])
        colsT = place("colsT", [P, KD, TAPS + 3])
        skT = place("skT", [P, 2, NKEYS])
        cond = place("cond", [P, KD])
        pos_i = place("pos_i", [P, NB], I32)
        pos_f = place("pos_f", [P, NB])
        NS = NB * RET_HEADS
        stat = place("stat", [P, NS, 6])
        mv = place("mv", [P, NS, 2])
        n_v, n_s, n_y, n_t = (place(f"n_{n}", [P, NS]) for n in "vsyt")
        hot_cols = place("hot_cols", [P, 3, 2 * GT])
        experts = place("experts", [P, NPAIR], U32)
        expert_u, expert_v = place("expert_u", [P, 2, NG], U32), place("expert_v", [P, 2, 2], U32)
        place = placer(R[6] + 24 * KB, R[6] + 32 * KB)
        vals = place("vals", [P, 2, NB, TOPK])
        idx_u = place("idx_u", [P, 2, NB, TOPK], U32)
        idx_f = place("idx_f", [P, 2, NB, TOPK])
        top = place("top", [P, NB, TOPK])
        pos_u = place("pos_u", [P, NB, TOPK], U32)
        pick_u = place("pick_u", [P, 2, NB, TOPK], U32)
        pick_f = place("pick_f", [P, 2, NB, TOPK])
        found = place("found", [P, 2, NB, TOPK])
        pair_sum = place("pair_sum", [P, NB * PEER_HEADS])

        HP = RET_HEADS * P
        causal = tab[:, 0:HP].rearrange("p (h i) -> p h i", h=RET_HEADS)
        decay = tab[:, HP:2 * HP].rearrange("p (h i) -> p h i", h=RET_HEADS)
        ident = tab[:, 2 * HP:2 * HP + P]
        inv_freq = tab[:, 2 * HP + P:NT - P]
        iota = tab[:, NT - P:NT]
        acts_dram = nc.dram_tensor("acts_dram", [TILES, P, TD], F32, kind="Internal").ap()
        routes_dram = nc.dram_tensor("routes_dram", [TILES, P, TD], F32, kind="Internal").ap()
        ps = ctx.enter_context(nc.psum_tensor("ps", [P, 8, NC], F32))

        tab_in, c_in, x_loaded, b_ada_in, pos_in = (sem(n) for n in ("tab_in", "c_in", "x_loaded", "b_ada_in", "pos_in"))
        cols_in, sub_in, row_in, x_again = (sem(n) for n in ("cols_in", "sub_in", "row_in", "x_again"))
        ada_in = [sem("ada_in0"), sem("ada_in1")]
        w_loaded = [sem("w_loaded0"), sem("w_loaded1")]
        tile_loaded = [sem(f"tile_loaded{i}") for i in range(RAW)]
        weighted_in = [sem(f"weighted_in{i}") for i in range(RAW)]
        zeroed, silu_c, ada_used = sem("zeroed"), sem("silu_c"), sem("ada_used")
        w_high, w_low, half_done = sem("w_high"), sem("w_low"), sem("half_done")
        bank_ready = sem("bank_ready")
        bank_free = [sem(f"bank_free{i}") for i in range(4)]
        job_ready = sem("job_ready")
        job_free = [sem(f"job_free{i}") for i in range(4)]
        dve_steps, conv_steps = sem("dve_steps"), sem("conv_steps")
        sumsq, var_ready, std_ready = sem("sumsq"), sem("var_ready"), sem("std_ready")
        tokens_ready, high_ready = sem("tokens_ready"), sem("high_ready")
        gate_written, gain_applied, row_used = sem("gate_written"), sem("gain_applied"), sem("row_used")
        glu_zero, angles, sines, rotated = sem("glu_zero"), sem("angles"), sem("sines"), sem("rotated")
        conv_done, centered, squared, y_ready, y_silu, y_high, y_low = (
            sem(n) for n in ("conv_done", "centered", "squared", "y_ready", "y_silu", "y_high", "y_low"))
        merged, x1_ready = sem("merged"), sem("x1_ready")
        query_ready, scores_ready, scores_copied = sem("query_ready"), sem("scores_ready"), sem("scores_copied")
        pairs_found, exp_in, exp_ready, pairs_ready, pairs_turned = (
            sem(n) for n in ("pairs_found", "exp_in", "exp_ready", "pairs_ready", "pairs_turned"))
        hot_ready, routes_ready, routes_staged = sem("hot_ready"), sem("routes_ready"), sem("routes_staged")
        stage_written = sem("stage_written")
        tile_high, tile_low, tile_used = sem("tile_high"), sem("tile_low"), sem("tile_used")
        acts_ready = sem("acts_ready")
        acts_written = [sem("acts_written0"), sem("acts_written1")]
        g_loaded = [sem(f"g_loaded{i}") for i in range(NG)]
        g_free = [sem(f"g_free{i}") for i in range(NG)]
        experts_ready, index_copied, dots_done, dots_gelu = (
            sem(n) for n in ("experts_ready", "index_copied", "dots_done", "dots_gelu"))
        wt_ready, wt_high, wt_low = sem("wt_ready"), sem("wt_high"), sem("wt_low")
        out_ready, out_written = sem("out_ready"), sem("out_written")

        jobs = [("cols", 0), ("cols", 1), ("sub", 0)]
        jobs += [("hT", i) for i in range(2 * NB)] + [("ada", i) for i in range(2 * NB)]
        jobs += [("rot", i) for i in range(2 * NB)] + [("mean", 0), ("var", 0)]
        for h in range(RET_HEADS):
            jobs += [("scores", h, j) for j in range(NB)] + [("ret", h, g) for g in range(NB // 2)]
        jobs += [("mT", i) for i in range(2 * NB)] + [("h2T", i) for i in range(2 * NB)]
        JOB = {name: n for n, name in enumerate(jobs)}

        def job_bank(*job):
            return ps[:, 4 + JOB[job] % 4, :]

        def job_may_start(pe, *job):
            if JOB[job] >= 4:
                pe.wait_ge(job_free[JOB[job] % 4], JOB[job] // 4)

        def job_is_ready(eng, *job):
            eng.wait_ge(job_ready, JOB[job] + 1)

        def job_freed(*job):
            return job_free[JOB[job] % 4]

        def job_is_read(eng, *job):
            eng.wait_ge(job_free[JOB[job] % 4], JOB[job] // 4 + 1)

        GLU_COL = QKV + 2 * D
        N_GLU, N_TOK = 2 * D // NC, (w_in.shape[2] - 2 * D) // NC
        N_LOW = GLU_COL // NC
        PW = 1 + N_GLU + N_TOK
        WO = PW + D // NC
        WQ = WO + D // NC
        N_WQ = w_peer_q.shape[2] // NC
        N_CH = WQ + N_WQ
        GATE_R = 1 + N_GLU + N_LOW
        GATE_C = GATE_R + D // NC
        w_in_v, w_pw_v, w_out_v, w_q_v = (w[0].rearrange("(k p) n -> p k n", p=P)
                                          for w in (w_in, w_pw2, w_out, w_peer_q))
        w_ada_v = w_ada[0].rearrange("(p j) n -> p j n", j=KD)

        def bank_is_read(eng, ch, i):
            eng.wait_ge(bank_free[i], ch + 1)

        block = ctx.enter_context(nc.Block())

        @block.sync
        def _(sp):
            def weight_unit(view, col, unit, half, first=False):
                if not first:
                    sp.wait_ge(w_low, unit - 1)
                sp.dma_start(w_raw[:, half], view[:, HU * half:HU * half + HU, bass.ds(col, NC)]).then_inc(w_loaded[half], 16)

            def ada_unit(a):
                part, j = divmod(a, KD)
                if a >= 2:
                    sp.wait_ge(ada_used, a - 1)
                sp.dma_start(ada_w[:, a % 2], w_ada_v[:, j, part * 2 * D:(part + 1) * 2 * D]).then_inc(ada_in[a % 2], 16)

            sp.dma_start(cond, c.rearrange("a (p j) -> p (a j)", j=KD)).then_inc(c_in, 16)
            for a in range(KD):
                ada_unit(a)
            for ch in range(N_GLU):
                for half in range(2):
                    u = 2 * ch + half
                    weight_unit(w_in_v, GLU_COL + ch * NC, u, half, first=u < 2)
                    ada_unit(KD + 2 * u)
                    ada_unit(KD + 2 * u + 1)
            with sp.Fori(0, N_LOW) as ch:
                for half in range(2):
                    weight_unit(w_in_v, ch * NC, ch * 2 + (2 * N_GLU + half), half)
            with sp.Fori(0, N_TOK - N_LOW) as ch:
                for half in range(2):
                    weight_unit(w_in_v, ch * NC + (GLU_COL + 2 * D), ch * 2 + (2 * (N_GLU + N_LOW) + half), half)
            for n, view in enumerate((w_pw_v, w_out_v)):
                for ch in range(D // NC):
                    for half in range(2):
                        weight_unit(view, ch * NC, 2 * (N_GLU + N_TOK + 2 * n + ch) + half, half)
                if n == 0:
                    sp.wait_ge(rotated, NB)
                    sp.dma_start(x1, x[0].rearrange("(b p) d -> p b d", p=P)).then_inc(x_again, 16)
            with sp.Fori(0, N_WQ) as ch:
                for half in range(2):
                    weight_unit(w_q_v, ch * NC, ch * 2 + (2 * (WQ - 1) + half), half)

            def load_tile(table, tile, raw, n, first=False):
                if not first:
                    sp.wait_ge(tile_low, n - (RAW - 1))
                sp.dma_start(tile_raw[raw], table[tile]).then_inc(tile_loaded[raw], 16)

            def write_acts(n, slot):
                sp.wait_ge(acts_ready, n + 1)
                sp.dma_start(acts_dram[n], acts[:, slot]).then_inc(acts_written[slot], 16)

            job_is_ready(sp, "h2T", 2 * NB - 1)
            for raw in range(2):
                load_tile(peer_uT, raw, raw, raw, first=True)
            sp.wait_ge(scores_ready, 4 * (N_WQ - 1) + 1)
            for raw in range(2, RAW):
                load_tile(peer_uT, raw, raw, raw, first=True)
            with sp.Fori(0, TILES // RAW - 1) as four:
                for j in range(RAW):
                    load_tile(peer_uT, four * RAW + (RAW + j), j, four * RAW + (RAW + j))
                    write_acts(four * RAW + j, j % 2)
            v_view = peer_v[0].rearrange("(t p) (k e) -> t p k e", p=P, k=KD)

            def load_weighted(m, slot, first=False):
                if not first:
                    sp.wait_ge(wt_ready, m - (RAW - 1))
                sp.dma_start(acts_in[:, slot], acts_dram[m]).then_inc(weighted_in[slot], 16)
                sp.dma_start(routes_in[:, slot], routes_dram[m]).then_inc(weighted_in[slot], 16)

            for j in range(RAW):
                load_tile(v_view, j, j, TILES + j)
                write_acts(TILES - RAW + j, j % 2)
            sp.wait_ge(stage_written, 16 * PIECES * ND)
            for s in range(2):
                sp.wait_ge(acts_written[s], 16 * TILES // 2)
            for slot in range(RAW):
                load_weighted(slot, slot, first=True)
            with sp.Fori(1, TILES // RAW) as four:
                for j in range(RAW):
                    load_weighted(four * RAW + j, j)
                    load_tile(v_view, four * RAW + j, j, four * RAW + (TILES + j))
            out_v = out[0].rearrange("(b p) d -> p b d", p=P)
            for b in range(NB):
                sp.wait_ge(out_ready, b + 1)
                sp.dma_start(out_v[:, b], out_buf[:, b]).then_inc(out_written, 16)
            sp.wait_ge(out_written, 16 * NB)

        @block.gpsimd
        def _(pool):
            pool.memset(ada_acc1, 0.0).then_inc(zeroed, 1)
            pool.memset(ada_acc2, 0.0).then_inc(zeroed, 1)
            pool.memset(cols, 0.0).then_inc(zeroed, 1)
            pool.memset(ones, 1.0).then_inc(zeroed, 1)
            pool.memset(glu[:, :, 0:PAD], 0.0).then_inc(glu_zero, 1)

            def low_part(u, half):
                pool.wait_ge(w_high, u + 1)
                pool.tensor_tensor(w_lo[:, half], w_raw[:, half], w_hi[:, half].bitcast(F32),
                                   ALU.subtract).then_inc(w_low, 1)

            low_part(0, 0)
            low_part(1, 1)
            with pool.Fori(1, GATE_R) as ch:
                for half in range(2):
                    low_part(ch * 2 + half, half)
            for ch in range(GATE_R, WQ):
                low_part(2 * ch, 0)
                if ch < GATE_C:
                    for b in range(NB):
                        n = (ch - GATE_R) * NB + b
                        pool.wait_ge(gate_written, n + 1)
                        g = ret_gate[:, b, bass.ds((ch - GATE_R) * NC, NC)]
                        pool.tensor_tensor(g, g, gate_tmp[:, b], ALU.mult).then_inc(bank_free[b], 1)
                low_part(2 * ch + 1, 1)
                if ch == GATE_C:
                    pool.wait_ge(row_in, 32)
                    for b in range(NB):
                        bank_is_read(pool, GATE_C - 1, b)
                        pool.tensor_tensor(ret_gate[:, b], ret_gate[:, b], row, ALU.mult).then_inc(gain_applied, 1)

            with pool.Fori(WQ, N_CH - 1) as ch:
                for half in range(2):
                    low_part(ch * 2 + half, half)

            def tile_low_part(n, raw):
                pool.wait_ge(tile_high, n + 1)
                pool.tensor_tensor(by_k(tile_lo[:, raw % 2]), tile_raw[raw], by_k(tile_hi[:, raw % 2].bitcast(F32)),
                                   ALU.subtract).then_inc(tile_low, 1)

            def gather(table, slot, index, free):
                wait_apart(pool, g_free[slot], free, glu_zero)
                pool.indirect_dma_start(out=gathered[slot], out_offset=None, in_=table,
                                        in_offset=bass.IndirectOffsetOnAxis(ap=index, axis=0)
                                        ).then_inc(g_loaded[slot], 16)

            def u_round(r, buf, tile, raw, slots=NG, first=False):
                for slot in range(slots if not first else 0):
                    wait_apart(pool, g_loaded[slot], r * 16 - 16, glu_zero)
                pool.tensor_copy(expert_u[:, buf, 0:slots], experts[:, bass.ds(r * NG, slots)]).then_inc(index_copied, 1)
                tile_low_part(tile, raw)
                wait_apart(pool, index_copied, r + 1, glu_zero)
                for slot in range(slots):
                    if slot == 1:
                        tile_low_part(tile + 1, raw + 1)
                    gather(peer_u[0], slot, expert_u[:, buf, slot:slot + 1], r + 1)

            with pool.Fori(0, W_TILE // RAW) as four:
                for j in range(RAW):
                    tile_low_part(four * RAW + j, j)
            pool.wait_ge(experts_ready, 1)
            for buf in range(2):
                u_round(buf, buf, W_TILE + 2 * buf, 2 * buf, first=True)
            with pool.Fori(1, G_BODY // 2) as two:
                for buf in range(2):
                    u_round(two * 2 + buf, buf, two * RAW + (W_TILE + 2 * buf), 2 * buf)
            u_round(G_BODY, 0, W_TILE + 2 * G_BODY, 0, slots=G_REST)
            for n in range(W_TILE + 2 * G_BODY + 2, TILES):
                tile_low_part(n, n % RAW)
            USED = G_BODY + 1

            def v_round(r, buf, tile, raw):
                for slot in range(2):
                    wait_apart(pool, g_loaded[slot], r * 16 + (USED - 1) * 16, glu_zero)
                pool.tensor_copy(expert_v[:, buf], experts[:, bass.ds(r * 2, 2)]).then_inc(index_copied, 1)
                for slot in range(2):
                    tile_low_part(tile + slot, raw + slot)
                    if slot == 0:
                        wait_apart(pool, index_copied, r + (USED + 1), glu_zero)
                    gather(peer_v[0], slot, expert_v[:, buf, slot:slot + 1], r + (USED + 1))

            assert G_REST == 2 and TILES == NPAIR and G_BODY % 2 == 0
            with pool.Fori(0, TILES // RAW) as two:
                for buf in range(2):
                    v_round(two * 2 + buf, buf, two * RAW + (TILES + 2 * buf), 2 * buf)

        @block.scalar
        def _(act):
            act.dma_start(tab, tables).then_inc(tab_in, 16)
            act.dma_start(x_in, x[0].rearrange("(b p) d -> p b d", p=P)).then_inc(x_loaded, 16)
            act.dma_start(row, norm_mix_gain[0].partition_broadcast(P)).then_inc(row_in, 16)
            act.dma_start(sub_raw[:, 0], peer_subkeys1[0]).then_inc(sub_in, 16)
            act.dma_start(sub_raw[:, 1], peer_subkeys2[0]).then_inc(sub_in, 16)
            act.dma_start(pos_i, positions[0].rearrange("(b p) -> p b", p=P),
                          allow_slow_non_contiguous=True).then_inc(pos_in, 16)
            act.wait_ge(zeroed, 3)
            act.dma_start(ada_acc1[0:1, :], b_ada[:, 0:2 * D]).then_inc(b_ada_in, 16)
            act.dma_start(ada_acc2[0:1, :], b_ada[:, 2 * D:6 * D]).then_inc(b_ada_in, 16)
            act.dma_start(cols[0:TAPS, :], w_dw[0, :, 0, :]).then_inc(cols_in, 16)
            for n, v in enumerate((b_dw, conv_ln_gain, conv_ln_bias)):
                act.dma_start(cols[TAPS + n:TAPS + n + 1, :], v).then_inc(cols_in, 16)
            act.wait_ge(c_in, 16)
            act.activation(cond, cond, ACT.Silu).then_inc(silu_c, 1)
            act.wait_ge(x_loaded, 16)
            for b in range(NB):
                if b:
                    act.wait_ge(sumsq, b)
                act.activation(junk, x_in[:, b], ACT.Square, accum_out=n_s[:, b:b + 1]).then_inc(sumsq, 1)
            for i in range(2):
                job_is_ready(act, "cols", i)
                act.activation(colsT[:, 4 * i:4 * i + 4, :],
                               job_bank("cols", i).rearrange("p (a b) -> p a b", a=4)[:, :, 0:TAPS + 3],
                               ACT.Copy).then_inc(job_freed("cols", i), 1)
            job_is_ready(act, "sub", 0)
            act.activation(skT.rearrange("p a b -> p (a b)"), job_bank("sub", 0)[:, 0:2 * P],
                           ACT.Copy).then_inc(job_freed("sub", 0), 1)

            def square_root(n, dst, src):
                act.wait_ge(var_ready, n)
                act.activation(dst, src, ACT.Sqrt).then_inc(std_ready, 1)

            square_root(1, n_s[:, 0:NB], n_v[:, 0:NB])
            for i in range(2):
                act.wait_ge(bank_ready, i + 1)
                act.activation(shift1[:, i * NC:(i + 1) * NC], ps[:, i], ACT.Copy).then_inc(bank_free[i], 1)

            def transposed_high(kind, dst):
                for n in range(2 * NB):
                    b, half = divmod(n, 2)
                    job_is_ready(act, kind, n)
                    act.activation(dst[:, HU * half:HU * half + HU, b * P:(b + 1) * P],
                                   job_bank(kind, n).rearrange("p (a b) -> p a b", a=HU),
                                   ACT.Copy).then_inc(high_ready, 1)

            def weight_high(ch, half, first=False):
                act.wait_ge(w_loaded[half], 16 * ch)
                if half == 0 and not first:
                    act.wait_ge(half_done, ch - 1)
                if half == 1 and not first:
                    act.wait_ge(bank_ready, 4 * ch)
                act.activation(w_hi[:, half], w_raw[:, half], ACT.Copy).then_inc(w_high, 1)

            transposed_high("hT", hT_hi)
            weight_high(1, 0, first=True)
            weight_high(1, 1, first=True)
            for ch in range(1, PW):
                weight_high(ch + 1, 0)
                k = ch - 1 - N_GLU
                for i in range(4):
                    func, half = ACT.Copy, slice(k % 2 * NC, k % 2 * NC + NC)
                    if ch <= N_GLU // 2:
                        dst = glu[:, 4 * (ch - 1) + i, PAD:PAD + T]
                        act.wait_ge(glu_zero, 1)
                    elif ch <= N_GLU:
                        dst, func = conv[:, 4 * (ch - 1 - N_GLU // 2) + i], ACT.Sigmoid
                    elif k < 2:
                        dst = qk_raw[:, i, half]
                    elif k < 4:
                        dst = val[:, i, half]
                    elif k < 6:
                        dst, func = ret_gate[:, i, half], ACT.Silu
                    elif ch < GATE_C:
                        dst, func = gate_tmp[:, i], ACT.Sigmoid
                    else:
                        dst, func = conv_gate[:, i, half], ACT.Sigmoid
                    act.wait_ge(bank_ready, 4 * ch + i + 1)
                    branch = GATE_R <= ch < GATE_C
                    if branch and ch > GATE_R:
                        bank_is_read(act, ch - 1, i)
                    act.activation(dst, ps[:, i], func).then_inc(gate_written if branch else bank_free[i], 1)
                weight_high(ch + 1, 1)
                if ch == N_GLU:
                    for i in range(2 * NB):
                        job_is_ready(act, "ada", i)
                        act.activation(mod[:, i // 2, i % 2 * NC:i % 2 * NC + NC], job_bank("ada", i),
                                       ACT.Copy).then_inc(job_freed("ada", i), 1)
                    act.wait_ge(row_used, 1)
                    act.dma_start(row, ret_gn_gain[0].partition_broadcast(P)).then_inc(row_in, 16)
            act.wait_ge(angles, 2)
            act.activation(sin_, ang, ACT.Sin).then_inc(sines, 1)
            act.activation(cos_, rest, ACT.Sin).then_inc(sines, 1)
            for n in range(2 * NB):
                b, half = divmod(n, 2)
                job_is_ready(act, "rot", n)
                act.activation((kT if half else qT)[:, :, b * P:(b + 1) * P],
                               job_bank("rot", n).rearrange("p (a b) -> p a b", a=RET_HEADS),
                               ACT.Copy).then_inc(job_freed("rot", n), 1)
            for t in range(KD):
                act.wait_ge(centered, t + 1)
                if t >= 2:
                    act.wait_ge(conv_done, t - 1)
                act.activation(squares[:, t % 2], conv[:, t], ACT.Square).then_inc(squared, 1)
            square_root(2, cv_s, cv_v)
            job_is_ready(act, "var", 0)
            for h in range(RET_HEADS):
                for g in range(NB // 2):
                    job_is_ready(act, "ret", h, g)
                    act.activation(retn[:, 2 * g:2 * g + 2, h * DV:(h + 1) * DV],
                                   job_bank("ret", h, g).rearrange("p (a b) -> p a b", a=2),
                                   ACT.Copy).then_inc(job_freed("ret", h, g), 1)
            for t in range(KD):
                act.wait_ge(y_ready, t + 1)
                act.activation(conv[:, t], conv[:, t], ACT.Silu, bias=colsT[:, t, TAPS + 2:TAPS + 3],
                               scale=colsT[:, t, TAPS + 1:TAPS + 2]).then_inc(y_silu, 1)
                act.wait_ge(y_silu, t + 1)
                act.activation(hT_hi[:, t], conv[:, t], ACT.Copy).then_inc(y_high, 1)
            square_root(3, n_s, n_v)
            weight_high(PW + 1, 0)
            weight_high(PW + 1, 1)
            act.wait_ge(gain_applied, NB)
            act.dma_start(row, norm_ffn_gain[0].partition_broadcast(P)).then_inc(row_in, 16)
            weight_high(WO, 0)
            weight_high(WO, 1)
            transposed_high("mT", hT_hi)
            weight_high(WO + 1, 0)
            weight_high(WO + 1, 1)
            weight_high(WQ, 0)
            weight_high(WQ, 1)
            for b in range(NB):
                act.wait_ge(x1_ready, (D // NC - 1) * NB + b + 1)
                act.activation(retn[:, b], x1[:, b], ACT.Square, accum_out=n_s[:, b:b + 1]).then_inc(sumsq, 1)
            square_root(4, n_s[:, 0:NB], n_v[:, 0:NB])
            act.wait_ge(row_used, 2)
            act.dma_start(row, final_norm_gain.partition_broadcast(P)).then_inc(row_in, 16)
            transposed_high("h2T", hT_hi)

            def query_copy(c, first=False):
                for i in range(4):
                    act.wait_ge(bank_ready, c * 4 + (4 * WQ + i + 1))
                    if not first:
                        act.wait_ge(scores_ready, c * 4)
                    act.activation(queryT[:, i], ps[:, i], ACT.Copy).then_inc(bank_free[i], 1)

            def score_copy(c):
                for i in range(4):
                    act.wait_ge(scores_ready, c * 4 + (i + 1))
                    act.activation(scores[:, bass.ds(c * 4 + i, 1), :].rearrange("p o t -> p (o t)"), ps[:, 4 + i],
                                   ACT.Copy).then_inc(scores_copied, 1)

            weight_high(WQ + 1, 0)
            query_copy(0, first=True)
            weight_high(WQ + 1, 1)
            with act.Fori(1, N_WQ - 1) as c:
                weight_high(c + (WQ + 1), 0)
                query_copy(c)
                weight_high(c + (WQ + 1), 1)
                score_copy(c - 1)
            query_copy(N_WQ - 1)
            score_copy(N_WQ - 2)

            def tile_split(n, raw, use):
                act.wait_ge(tile_loaded[raw], use * 16 + 16)
                if not isinstance(n, int) or n >= 2:
                    act.wait_ge(tile_used, n - 1)
                act.activation(by_k(tile_hi[:, raw % 2]), tile_raw[raw], ACT.Copy).then_inc(tile_high, 1)

            def expert_gelu(n, slot, first=False):
                act.wait_ge(tile_used, n + 1)
                if not first:
                    act.wait_ge(acts_written[slot], (n - slot) * 8)
                act.activation(acts[:, slot], ps[:, 4 + slot, 0:TD], ACT.Gelu_apprx_tanh).then_inc(acts_ready, 1)

            def split_ahead(four, j):
                tile_split(four * RAW + (j + 2), (j + 2) % RAW, four + (j + 2) // RAW)

            def tile_step(four, j, first=False):
                split_ahead(four, j)
                expert_gelu(four * RAW + j, j % 2, first)

            def stage_routes(g, slot, at_token):
                act.wait_ge(routes_ready, g + 1)
                for q in range(2):
                    dst = stage[:, :, bass.ds(at_token + q * GT // 2, GT // 2)]
                    ins = act.activation(dst, ps[:, 2 * slot + q].rearrange("p (t k) -> p k t", k=NKEYS), ACT.Copy)
                ins.then_inc(routes_staged, 1)

            for n in range(2):
                tile_split(n, n, 0)
            score_copy(N_WQ - 1)
            for j in range(RAW):
                tile_step(0, j, first=j < 2)
            with act.Fori(1, W_TILE // RAW) as four:
                for j in range(RAW):
                    tile_step(four, j)
            act.wait_ge(exp_in, 1)
            weights = pairs[:, WT].rearrange("p b n -> p (b n)")
            act.activation(weights, weights, ACT.Exp).then_inc(exp_ready, 1)

            def routes_block(b, first=False):
                if not first:
                    act.wait_ge(stage_written, b * (16 * PIECES))
                with act.Fori(0, GB // RAW) as i:
                    for j in range(RAW):
                        tile_step(i + b * (TB // RAW) + W_TILE // RAW, j)
                        stage_routes(b * GB + i * RAW + j, j % 2, i * (RAW * GT) + j * GT)
                act.wait_ge(routes_staged, b * GB + GB)
                for q in range(PIECES):
                    keys = slice(q * NKEYS // PIECES, (q + 1) * NKEYS // PIECES)
                    act.dma_start(routes_dram[keys, :, bass.ds(b * P, P)].rearrange("a p t -> p a t"),
                                  stage[:, keys]).then_inc(stage_written, 16)
                with act.Fori(GB // RAW, TB // RAW) as i:
                    for j in range(RAW):
                        tile_step(i + b * (TB // RAW) + W_TILE // RAW, j)

            routes_block(0, first=True)
            with act.Fori(1, ND) as b:
                routes_block(b)
            with act.Fori((W_TILE + ND * TB) // RAW, TILES // RAW) as four:
                for j in range(RAW):
                    tile_step(four, j)

            def weighted_split(m, slot):
                act.wait_ge(wt_ready, m + 1)
                act.activation(wt_hi[:, slot], weighted[:, slot], ACT.Copy).then_inc(wt_high, 1)

            for slot in range(2):
                weighted_split(slot, slot)
            act.wait_ge(dots_done, 1)
            act.activation(dots, dots, ACT.Gelu_apprx_tanh).then_inc(dots_gelu, 1)
            with act.Fori(0, TILES // RAW - 1) as four:
                for j in range(RAW):
                    split_ahead(four + TILES // RAW, j)
                    weighted_split(four * RAW + (j + 2), j % 2)
            for j in range(RAW - 2):
                split_ahead(2 * TILES // RAW - 1, j)
                weighted_split(TILES - RAW + j + 2, j % 2)

            for b in range(NB):
                act.wait_ge(x1_ready, D // NC * NB + b + 1)
                act.activation(squares_out[:, b], x1[:, b], ACT.Square, accum_out=n_s[:, b:b + 1]).then_inc(sumsq, 1)
            square_root(5, n_s[:, 0:NB], n_v[:, 0:NB])

        @block.tensor
        def _(pe):
            def product3(dst, stat_, moving, start, stop):
                (sh, sl), (mh, ml) = stat_, moving
                pe.matmul(dst, sh, mh, start=start, stop=False)
                pe.matmul(dst, sh, ml, start=False, stop=False)
                return pe.matmul(dst, sl, mh, start=False, stop=stop)

            def both(hi, lo, *index):
                return hi[index], lo[index]

            def chunk(ch, tokens_stationary):
                for half in range(2):
                    pe.wait_ge(w_low, ch * 2 + (half - 1))
                    for i in range(4):
                        if half == 0:
                            pe.wait_ge(bank_free[i], ch)
                        for k in range(HU):
                            tok = (slice(None), HU * half + k, slice(i * P, (i + 1) * P) if tokens_stationary else slice(None))
                            w = (slice(None), half, k, slice(None) if tokens_stationary else slice(i * P, (i + 1) * P))
                            tok, w = both(hT_hi, hT_lo, *tok), both(w_hi, w_lo, *w)
                            a, b = (tok, w) if tokens_stationary else (w, tok)
                            mm = product3(ps[:, i], a, b, half == 0 and k == 0, half == 1 and k == HU - 1)
                        if half == 1:
                            mm.then_inc(bank_ready, 1)
                    if half == 0:
                        mm.then_inc(half_done, 1)

            def transposes(job, sources):
                job_may_start(pe, *job)
                for n, src in enumerate(sources):
                    mm = pe.transpose(job_bank(*job)[:, n * P:(n + 1) * P], src, ident)
                mm.then_inc(job_ready, 1)

            def token_transposes(kind, src, ready):
                for n in range(2 * NB):
                    b, half = divmod(n, 2)
                    ready(b, half)
                    transposes((kind, n), [src[:, b, (HU * half + k) * P:(HU * half + k + 1) * P] for k in range(HU)])

            pe.wait_ge(tab_in, 16)
            pe.wait_ge(zeroed, 4)
            pe.wait_ge(cols_in, 64)
            for i in range(2):
                transposes(("cols", i), [cols[:, (4 * i + k) * P:(4 * i + k + 1) * P] for k in range(4)])
            pe.wait_ge(sub_in, 32)
            transposes(("sub", 0), [sub_raw[:, 0], sub_raw[:, 1]])
            pe.wait_ge(ada_used, KD)
            for i in range(4):
                pe.matmul(ps[:, i], ones, ada_acc1[:, i * NC:(i + 1) * NC], start=True, stop=True).then_inc(bank_ready, 1)
            token_transposes("hT", x_in, lambda b, half: pe.wait_ge(tokens_ready, b + 1))
            job_is_read(pe, "hT", 6)
            job_is_read(pe, "hT", 7)
            with pe.Fori(1, 1 + N_GLU) as ch:
                chunk(ch, False)
            pe.wait_ge(ada_used, 3 * KD)
            for i in range(2 * NB):
                job_may_start(pe, "ada", i)
                pe.matmul(job_bank("ada", i), ones, ada_acc2[:, i * NC:(i + 1) * NC],
                          start=True, stop=True).then_inc(job_ready, 1)
            with pe.Fori(1 + N_GLU, PW) as ch:
                chunk(ch, True)
            for n in range(2 * NB):
                b, half = divmod(n, 2)
                pe.wait_ge(rotated, b + 1)
                transposes(("rot", n), [qk_rot[:, b, (RET_HEADS * half + h) * P:(RET_HEADS * half + h + 1) * P]
                                        for h in range(RET_HEADS)])
            job_may_start(pe, "mean", 0)
            pe.wait_ge(conv_steps, KD * TAPS)
            for t in range(KD):
                mm = pe.matmul(job_bank("mean", 0), ones, conv[:, t], start=t == 0, stop=t == KD - 1)
            mm.then_inc(job_ready, 1)
            job_may_start(pe, "var", 0)
            for t in range(KD):
                pe.wait_ge(squared, t + 1)
                mm = pe.matmul(job_bank("var", 0), ones, squares[:, t % 2], start=t == 0, stop=t == KD - 1)
                mm.then_inc(conv_done if t < KD - 1 else job_ready, 1)
            for n in range(2 * NB):
                job_is_read(pe, "rot", n)
            for h in range(RET_HEADS):
                for j in range(NB):
                    job_may_start(pe, "scores", h, j)
                    pe.matmul(job_bank("scores", h, j)[:, j * P:T], kT[:, h, j * P:(j + 1) * P], qT[:, h, j * P:T],
                              start=True, stop=True).then_inc(job_ready, 1)
                for g in range(NB // 2):
                    job_may_start(pe, "ret", h, g)
                    for j in range(2 * g + 2):
                        if 2 * g <= j or g == 0:
                            job_is_read(pe, "scores", h, j)
                    for bb in range(2):
                        b = 2 * g + bb
                        for j in range(b + 1):
                            mm = pe.matmul(job_bank("ret", h, g)[:, bb * DV:(bb + 1) * DV],
                                           ret_scores[:, j, b * P:(b + 1) * P], val[:, j, h * DV:(h + 1) * DV],
                                           start=j == 0, stop=j == b)
                    mm.then_inc(job_ready, 1)
            pe.wait_ge(y_low, KD)
            for ch in range(PW, WO):
                chunk(ch, True)
            token_transposes("mT", conv_gate, lambda b, half: pe.wait_ge(merged, half * NB + b + 1))
            job_is_read(pe, "mT", 6)
            job_is_read(pe, "mT", 7)
            for ch in range(WO, WQ):
                chunk(ch, True)
            token_transposes("h2T", h2, lambda b, half: pe.wait_ge(tokens_ready, NB + b + 1))
            job_is_read(pe, "h2T", 6)
            job_is_read(pe, "h2T", 7)
            def head_scores(c, first=False):
                for i in range(4):
                    bank_is_read(pe, c + WQ, i)
                    if not first:
                        pe.wait_ge(scores_copied, c * 4)
                    for b in range(NB):
                        mm = pe.matmul(ps[:, 4 + i, b * NKEYS:(b + 1) * NKEYS], queryT[:, i, b * P:(b + 1) * P],
                                       skT[:, i % 2], start=True, stop=True)
                    mm.then_inc(scores_ready, 1)

            chunk(WQ, False)
            chunk(WQ + 1, False)
            head_scores(0, first=True)
            with pe.Fori(2, N_WQ) as c:
                chunk(c + WQ, False)
                head_scores(c - 1)
            head_scores(N_WQ - 1)

            def expert_tile(n, slot, first=False):
                pe.wait_ge(tile_low, n + 1)
                if first:
                    pe.wait_ge(scores_copied, 4 * N_WQ)
                else:
                    pe.wait_ge(acts_ready, n - 1)
                for k in range(KD):
                    mm = product3(ps[:, 4 + slot, 0:TD], both(tile_hi, tile_lo, slice(None), slot, slice(k * P, (k + 1) * P)),
                                  both(hT_hi, hT_lo, slice(None), k, slice(0, TD)), k == 0, k == KD - 1)
                mm.then_inc(tile_used, 1)

            def routes_group(g, slot, first=False):
                pe.wait_ge(hot_ready, g + 1)
                if not first:
                    pe.wait_ge(routes_staged, g - 1)
                for t in range(GT):
                    mm = pe.matmul(ps[:, 2 * slot + t * 2 // GT, t % (GT // 2) * P:(t % (GT // 2) + 1) * P],
                                   hot[:, slot, t, 0], hot[:, slot, t, 1], start=True, stop=True)
                mm.then_inc(routes_ready, 1)

            for n in range(2):
                expert_tile(n, n, first=True)
            with pe.Fori(1, W_TILE // 2) as i:
                for slot in range(2):
                    expert_tile(i * 2 + slot, slot)
            pe.wait_ge(pairs_ready, 1)
            for i in range(3):
                for b in range(ND):
                    mm = pe.transpose(ps[:, i, b * P:(b + 1) * P], pairs[:, i, b], ident)
            mm.then_inc(pairs_turned, 1)
            def routes_block(b, first=False):
                if first:
                    for slot in range(2):
                        expert_tile(W_TILE + slot, slot)
                        routes_group(slot, slot, first=True)
                with pe.Fori(1 if first else 0, GB // 2) as i:
                    for slot in range(2):
                        expert_tile(b * TB + i * 2 + (W_TILE + slot), slot)
                        routes_group(b * GB + i * 2 + slot, slot)
                with pe.Fori(GB // 2, TB // 2) as i:
                    for slot in range(2):
                        expert_tile(b * TB + i * 2 + (W_TILE + slot), slot)

            routes_block(0, first=True)
            with pe.Fori(1, ND) as b:
                routes_block(b)
            with pe.Fori((W_TILE + ND * TB) // 2, TILES // 2) as i:
                for slot in range(2):
                    expert_tile(i * 2 + slot, slot)

            def value_tile(m, slot, first=False, last=False):
                pe.wait_ge(wt_low, m + 1)
                pe.wait_ge(tile_low, m + (TILES + 1))
                for b in range(ND):
                    for half in range(D // NC):
                        mm = product3(ps[:, b * D // NC + half],
                                      both(wt_hi, wt_lo, slice(None), slot, slice(b * P, (b + 1) * P)),
                                      both(tile_hi, tile_lo, slice(None), slot, slice(half * NC, (half + 1) * NC)),
                                      first, last)
                mm.then_inc(tile_used, 1)

            pe.wait_ge(acts_ready, TILES)
            pe.wait_ge(routes_staged, GROUPS)
            value_tile(0, 0, first=True)
            value_tile(1, 1)
            with pe.Fori(1, TILES // 2 - 1) as i:
                for slot in range(2):
                    value_tile(i * 2 + slot, slot)
            value_tile(TILES - 2, 0)
            value_tile(TILES - 1, 1, last=True)

        @block.vector
        def _(dve):
            st = Steps(dve, dve_steps)

            def root_reciprocal(n, v, s, y, t):
                dve.wait_ge(std_ready, n)
                st.do(dve.reciprocal(y, s))
                st.do(dve.tensor_tensor(t, v, y, ALU.mult))
                st.do(dve.tensor_tensor(t, t, y, ALU.mult))
                st.do(dve.tensor_scalar(t, t, -0.5, 1.5, ALU.mult, ALU.add))
                st.do(dve.tensor_tensor(y, y, t, ALU.mult))

            def token_variance(n):
                dve.wait_ge(sumsq, n * NB)
                dve.tensor_scalar(n_v[:, 0:NB], n_s[:, 0:NB], 1.0 / D, EPS, ALU.mult, ALU.add).then_inc(var_ready, 1)
                dve.wait_ge(var_ready, {1: 1, 2: 4, 3: 5}[n])

            def transposed_low(kind, dst_hi, dst_lo, before):
                for n in range(2 * NB):
                    b, half = divmod(n, 2)
                    dve.wait_ge(high_ready, before + n + 1)
                    part = (slice(None), slice(HU * half, HU * half + HU), slice(b * P, (b + 1) * P))
                    dve.tensor_tensor(dst_lo[part], job_bank(kind, n).rearrange("p (a b) -> p a b", a=HU),
                                      dst_hi[part].bitcast(F32), ALU.subtract).then_inc(job_freed(kind, n), 1)

            dve.wait_ge(silu_c, 1)
            dve.wait_ge(b_ada_in, 32)

            def ada_sum(a, acc):
                j = a % KD
                dve.wait_ge(ada_in[a % 2], 16 * (a // 2 + 1))
                dve.scalar_tensor_tensor(out=acc, in0=ada_w[:, a % 2], scalar=cond[:, j:j + 1], in1=acc,
                                         op0=ALU.mult, op1=ALU.add).then_inc(ada_used, 1)
                dve.wait_ge(ada_used, a + 1)

            for a in range(KD):
                ada_sum(a, ada_acc1)
            token_variance(1)
            root_reciprocal(1, n_v[:, 0:NB], n_s[:, 0:NB], n_y[:, 0:NB], n_t[:, 0:NB])
            dve.wait_ge(row_in, 16)
            for i in range(2):
                dve.wait_ge(bank_ready, 2 + i + 1)
                cols_i = slice(i * NC, (i + 1) * NC)
                dve.scalar_tensor_tensor(out=scale1[:, cols_i], in0=ps[:, 2 + i], scalar=1.0, in1=row[:, cols_i],
                                         op0=ALU.add, op1=ALU.mult).then_inc(bank_free[2 + i], 1)
                bank_is_read(dve, 0, i)
                bank_is_read(dve, 0, 2 + i)
            for b in range(NB):
                st.do(dve.scalar_tensor_tensor(out=x_in[:, b], in0=x_in[:, b], scalar=n_y[:, b:b + 1], in1=scale1,
                                               op0=ALU.mult, op1=ALU.mult))
                if b == 0:
                    dve.engine_nop().then_inc(row_used, 1)
                dve.tensor_tensor(x_in[:, b], x_in[:, b], shift1, ALU.add).then_inc(tokens_ready, 1)
            transposed_low("hT", hT_hi, hT_lo, 0)
            for a in range(KD, 3 * KD):
                ada_sum(a, ada_acc2[:, (a // KD - 1) * 2 * D:(a // KD) * 2 * D])

            for i in range(4):
                bank_is_read(dve, N_GLU, i)
            st.do(dve.tensor_tensor(glu[:, :, PAD:PAD + T], glu[:, :, PAD:PAD + T], conv, ALU.mult))
            job_is_read(dve, "cols", 0)
            job_is_read(dve, "cols", 1)
            for t in range(KD):
                dve.tensor_scalar(conv[:, t], glu[:, t, 0:T], colsT[:, t, 0:1], colsT[:, t, TAPS:TAPS + 1],
                                  ALU.mult, ALU.add).then_inc(conv_steps, 1)
            with dve.Fori(1, TAPS) as tap:
                for t in range(KD):
                    dve.wait_ge(conv_steps, tap * KD + (t + 1 - KD))
                    dve.scalar_tensor_tensor(out=conv[:, t], in0=glu[:, t, bass.ds(tap, T)],
                                             scalar=colsT[:, t, bass.ds(tap, 1)], in1=conv[:, t],
                                             op0=ALU.mult, op1=ALU.add).then_inc(conv_steps, 1)
            dve.wait_ge(conv_steps, KD * TAPS)

            dve.wait_ge(pos_in, 16)
            st.do(dve.tensor_copy(pos_f, pos_i))
            for b in range(NB):
                st.inc(dve.tensor_scalar(ang[:, b], inv_freq, pos_f[:, b:b + 1], None, ALU.mult))
            st.wait()
            st.do(dve.tensor_scalar(rest, ang, float(1 / (2 * np.pi)), ROUND_MAGIC, ALU.mult, ALU.add))
            st.do(dve.tensor_scalar(rest, rest, ROUND_MAGIC, None, ALU.subtract))
            for part in (TURN_1, TURN_2, TURN_3):
                st.do(dve.scalar_tensor_tensor(out=ang, in0=rest, scalar=-part, in1=ang, op0=ALU.mult, op1=ALU.add))
            dve.tensor_scalar(ang, ang, SIN_LIMIT, -SIN_LIMIT, ALU.min, ALU.max).then_inc(angles, 1)
            dve.wait_ge(angles, 1)
            st.do(dve.scalar_tensor_tensor(out=rest, in0=ang, scalar=-1.0, in1=ang, op0=ALU.mult, op1=ALU.max))
            dve.tensor_scalar(rest, rest, -1.0, float(np.pi / 2), ALU.mult, ALU.add).then_inc(angles, 1)
            dve.wait_ge(sines, 2)
            for i in range(4):
                bank_is_read(dve, 2 + N_GLU, i)
            for b in range(NB):
                raw = qk_raw[:, b].rearrange("p (h s d) -> p h s d", s=2, d=P // 2)
                rot = qk_rot[:, b].rearrange("p (h s d) -> p h s d", s=2, d=P // 2)
                first, second = raw[:, :, 0], raw[:, :, 1]
                cos_b, sin_b = (v[:, b].unsqueeze(1).broadcast_to([P, 2 * RET_HEADS, P // 2]) for v in (cos_, sin_))
                t0, t1 = (rot_tmp[:, i].rearrange("p (h d) -> p h d", d=P // 2) for i in range(2))
                st.inc(dve.tensor_tensor(rot[:, :, 0], first, cos_b, ALU.mult))
                st.inc(dve.tensor_tensor(t0, second, sin_b, ALU.mult))
                st.inc(dve.tensor_tensor(rot[:, :, 1], first, sin_b, ALU.mult))
                st.inc(dve.tensor_tensor(t1, second, cos_b, ALU.mult))
                st.wait()
                st.inc(dve.tensor_tensor(rot[:, :, 0], rot[:, :, 0], t0, ALU.subtract))
                st.wait()
                dve.tensor_tensor(rot[:, :, 1], rot[:, :, 1], t1, ALU.add).then_inc(rotated, 1)
                dve.wait_ge(rotated, b + 1)

            job_is_ready(dve, "mean", 0)
            for t in range(KD):
                ins = dve.scalar_tensor_tensor(out=conv[:, t], in0=job_bank("mean", 0), scalar=-1.0 / D, in1=conv[:, t],
                                               op0=ALU.mult, op1=ALU.add)
                ins.then_inc(centered if t < KD - 1 else job_freed("mean", 0), 1)
            job_is_read(dve, "mean", 0)
            dve.engine_nop().then_inc(centered, 1)
            job_is_ready(dve, "var", 0)
            dve.tensor_scalar(cv_v, job_bank("var", 0), 1.0 / D, EPS, ALU.mult, ALU.add).then_inc(job_freed("var", 0), 1)
            job_is_read(dve, "var", 0)
            dve.engine_nop().then_inc(var_ready, 1)
            root_reciprocal(2, cv_v, cv_s, cv_y, cv_t)
            for t in range(KD):
                dve.tensor_tensor(conv[:, t], conv[:, t], cv_y, ALU.mult).then_inc(y_ready, 1)

            for h in range(RET_HEADS):
                gamma = 1.0 - 2.0 ** (-5.0 - h)
                for j in range(NB):
                    job_is_ready(dve, "scores", h, j)
                    if h and j == 0:
                        job_is_read(dve, "ret", h - 1, 0)
                        job_is_read(dve, "ret", h - 1, 1)
                    bank = job_bank("scores", h, j)
                    for i in range(j, NB):
                        blk = slice(i * P, (i + 1) * P)
                        if i == j:
                            ins = dve.tensor_tensor(ret_scores[:, j, blk], bank[:, blk], causal[:, h], ALU.mult)
                        else:
                            ins = dve.scalar_tensor_tensor(out=ret_scores[:, j, blk], in0=bank[:, blk],
                                                           scalar=float(gamma ** (P * (i - j))), in1=decay[:, h],
                                                           op0=ALU.mult, op1=ALU.mult)
                    ins.then_inc(job_freed("scores", h, j), 1)
            for n in range(NS):
                b, h = divmod(n, RET_HEADS)
                job_is_read(dve, "ret", h, b // 2)
                st.inc(dve.bn_stats(stat[:, n], retn[:, b, h * DV:(h + 1) * DV]))
            st.wait()
            for n in range(NS):
                st.inc(dve.bn_aggr(mv[:, n], stat[:, n]))
            st.wait()
            dve.tensor_scalar(n_v, mv[:, :, 1], EPS, None, ALU.add).then_inc(var_ready, 1)
            dve.wait_ge(var_ready, 3)
            for t in range(KD):
                dve.wait_ge(y_high, t + 1)
                dve.tensor_tensor(hT_lo[:, t], conv[:, t], hT_hi[:, t].bitcast(F32), ALU.subtract).then_inc(y_low, 1)
            root_reciprocal(3, n_v, n_s, n_y, n_t)
            for n in range(NS):
                b, h = divmod(n, RET_HEADS)
                part = retn[:, b, h * DV:(h + 1) * DV]
                st.inc(dve.tensor_scalar(part, part, mv[:, n, 0:1], n_y[:, n:n + 1], ALU.subtract, ALU.mult))
            st.wait()
            dve.wait_ge(gain_applied, NB)
            for b in range(NB):
                st.inc(dve.tensor_tensor(retn[:, b], retn[:, b], ret_gate[:, b], ALU.mult))
            for i in range(2 * NB):
                job_is_read(dve, "ada", i)
            dve.wait_ge(row_in, 48)
            dve.scalar_tensor_tensor(out=mod[:, SCALE2], in0=mod[:, SCALE2], scalar=1.0, in1=row,
                                     op0=ALU.add, op1=ALU.mult).then_inc(row_used, 1)
            st.wait()
            for ch in range(PW, WO):
                for b in range(NB):
                    part = (slice(None), b, slice((ch - PW) * NC, (ch - PW + 1) * NC))
                    dve.wait_ge(bank_ready, 4 * ch + b + 1)
                    dve.tensor_tensor(conv_gate[part], ps[:, b], conv_gate[part], ALU.mult).then_inc(bank_free[b], 1)
                    bank_is_read(dve, ch, b)
                    dve.tensor_tensor(conv_gate[part], conv_gate[part], retn[part], ALU.add).then_inc(merged, 1)
            transposed_low("mT", hT_hi, hT_lo, 2 * NB)
            dve.wait_ge(x_again, 16)
            for ch in range(WO, WQ):
                for b in range(NB):
                    half = slice((ch - WO) * NC, (ch - WO + 1) * NC)
                    dve.wait_ge(bank_ready, 4 * ch + b + 1)
                    dve.tensor_tensor(retn[:, b, half], ps[:, b], mod[:, GATE1, half], ALU.mult).then_inc(bank_free[b], 1)
                    bank_is_read(dve, ch, b)
                    dve.tensor_tensor(x1[:, b, half], x1[:, b, half], retn[:, b, half], ALU.add).then_inc(x1_ready, 1)
            token_variance(2)
            root_reciprocal(4, n_v[:, 0:NB], n_s[:, 0:NB], n_y[:, 0:NB], n_t[:, 0:NB])
            dve.wait_ge(row_used, 2)
            for b in range(NB):
                st.do(dve.scalar_tensor_tensor(out=h2[:, b], in0=x1[:, b], scalar=n_y[:, b:b + 1], in1=mod[:, SCALE2],
                                               op0=ALU.mult, op1=ALU.mult))
                dve.tensor_tensor(h2[:, b], h2[:, b], mod[:, SHIFT2], ALU.add).then_inc(tokens_ready, 1)
            dve.wait_ge(tokens_ready, 2 * NB)
            transposed_low("h2T", hT_hi, hT_lo, 4 * NB)
            for slot in range(NG):
                dve.memset(yacc[:, slot * D // NG:(slot + 1) * D // NG], 0.0).then_inc(g_free[slot], 1)
            grid = [P, NB, TOPK, TOPK]

            def each(op):
                for half in range(2):
                    for b in range(NB):
                        op(half, b)

            def topk(h):
                wait_apart(dve, scores_copied, h * 2 + 2, sumsq)
                st.inc(dve.tensor_copy(work.rearrange("p a b n -> p a (b n)"), scores[:, bass.ds(h * 2, 2), :]))
                st.wait_apart()
                each(lambda a, b: st.inc(dve.max(vals[:, a, b, 0:8], work[:, a, b])))
                st.wait_apart()
                each(lambda a, b: st.inc(dve.max_index(idx_u[:, a, b, 0:8], vals[:, a, b, 0:8], work[:, a, b])))
                each(lambda a, b: st.inc(dve.match_replace(work[:, a, b], vals[:, a, b, 0:8], work[:, a, b], VERY_LOW)))
                st.wait_apart()
                each(lambda a, b: st.inc(dve.max(vals[:, a, b, 8:16], work[:, a, b])))
                st.wait_apart()
                each(lambda a, b: st.inc(dve.max_index(idx_u[:, a, b, 8:16], vals[:, a, b, 8:16], work[:, a, b])))
                for b in range(NB):
                    st.inc(dve.tensor_tensor(cand[:, b].rearrange("p (i j) -> p i j", i=TOPK),
                                             vals[:, 0, b].unsqueeze(2).broadcast_to([P, TOPK, TOPK]),
                                             vals[:, 1, b].unsqueeze(1).broadcast_to([P, TOPK, TOPK]), ALU.add))
                st.wait_apart()
                for b in range(NB):
                    st.inc(dve.max(top[:, b, 0:8], cand[:, b]))
                st.wait_apart()
                for b in range(NB):
                    st.inc(dve.max_index(pos_u[:, b, 0:8], top[:, b, 0:8], cand[:, b]))
                for b in range(NB):
                    st.inc(dve.match_replace(cand[:, b], top[:, b, 0:8], cand[:, b], VERY_LOW))
                st.wait_apart()
                for b in range(NB):
                    st.inc(dve.max(top[:, b, 8:16], cand[:, b]))
                st.wait_apart()
                for b in range(NB):
                    st.inc(dve.max_index(pos_u[:, b, 8:16], top[:, b, 8:16], cand[:, b]))
                st.inc(dve.tensor_tensor(pairs[:, WT, :, bass.ds(h * TOPK, TOPK)], top,
                                         top[:, :, 0:1].broadcast_to([P, NB, TOPK]), ALU.subtract))
                st.inc(dve.tensor_copy(idx_f, idx_u))
                st.wait()
                st.inc(dve.tensor_scalar(pick_u[:, 0], pos_u, 4, None, ALU.logical_shift_right))
                st.do(dve.tensor_scalar(pick_u[:, 1], pos_u, TOPK - 1, None, ALU.bitwise_and))
                st.do(dve.tensor_copy(pick_f, pick_u))
                flat = [P, NB * TOPK, TOPK]
                for a in range(2):
                    st.inc(dve.tensor_tensor(onehot[:, a], iota[:, 0:TOPK].unsqueeze(1).broadcast_to(flat),
                                             pick_f[:, a].rearrange("p b k -> p (b k)").unsqueeze(2).broadcast_to(flat),
                                             ALU.is_equal))
                st.wait()
                each(lambda a, b: st.inc(dve.tensor_tensor(
                    onehot[:, a, b * TOPK:(b + 1) * TOPK], onehot[:, a, b * TOPK:(b + 1) * TOPK],
                    idx_f[:, a, b].unsqueeze(1).broadcast_to([P, TOPK, TOPK]), ALU.mult)))
                st.wait_apart()
                for a, key in ((0, K1), (1, K2)):
                    st.inc(dve.tensor_reduce(pairs[:, key, :, bass.ds(h * TOPK, TOPK)],
                                             onehot[:, a].rearrange("p (b k) i -> p b k i", b=NB), AX_X, ALU.add))

            with dve.Fori(0, PEER_HEADS) as h:
                st.loop(h, 1 + 4 * 8 + 8 + NB + 5 * NB + 2 + 3 + 2 + 8 + 2)
                topk(h)
            st.end(PEER_HEADS)
            st.wait()
            dve.engine_nop().then_inc(exp_in, 1)
            dve.wait_ge(exp_ready, 1)
            by_head = pairs[:, WT].rearrange("p b (h k) -> p (b h) k", k=TOPK)
            st.do(dve.tensor_reduce(pair_sum, by_head, AX_X, ALU.add))
            st.do(dve.reciprocal(pair_sum, pair_sum))
            dve.tensor_tensor(by_head, by_head, pair_sum.unsqueeze(2).broadcast_to([P, NB * PEER_HEADS, TOPK]),
                              ALU.mult).then_inc(pairs_ready, 1)
            dve.scalar_tensor_tensor(out=experts, in0=pairs[:, K1, ND], scalar=float(NKEYS), in1=pairs[:, K2, ND],
                                     op0=ALU.mult, op1=ALU.add).then_inc(experts_ready, 1)
            dve.wait_ge(pairs_turned, 1)
            for i in range(3):
                st.inc(dve.tensor_copy(pairsT[:, i], ps[:, i, 0:TD]))
            st.wait()

            def hot_group(g, slot, first=False):
                if not first:
                    dve.wait_ge(routes_ready, g - 1)
                for t in range(GT):
                    col = slice(slot * GT + t, slot * GT + t + 1)
                    dve.tensor_scalar(hot[:, slot, t, 0], iota, hot_cols[:, K2, col], None, ALU.is_equal)
                    ins = dve.tensor_scalar(hot[:, slot, t, 1], iota, hot_cols[:, K1, col], hot_cols[:, WT, col],
                                            ALU.is_equal, ALU.mult)
                ins.then_inc(hot_ready, 1)

            def row_dots(i, slots):
                for slot in range(slots):
                    dve.wait_ge(g_loaded[slot], i * 16 + 16)
                    dve.tensor_tensor_reduce(gathered[slot], gathered[slot], h2[:, ND], 1.0, 0.0, ALU.mult, ALU.add,
                                             dots_now[:, slot:slot + 1]).then_inc(g_free[slot], 1)
                for slot in range(slots):
                    wait_apart(dve, g_free[slot], i + 2, sumsq)
                st.do(dve.tensor_copy(dots[:, bass.ds(i * NG, slots)], dots_now[:, 0:slots]))

            st.do(dve.tensor_copy(hot_cols, pairsT[:, :, 0:2 * GT]))
            for slot in range(2):
                hot_group(slot, slot, first=True)
            row_dots(0, NG)

            def hot_pair(r, b, i):
                wait_apart(dve, hot_ready, b * GB + i * 2, sumsq)
                st.do(dve.tensor_copy(hot_cols, pairsT[:, :, bass.ds(b * P + i * (2 * GT), 2 * GT)]))
                for slot in range(2):
                    hot_group(b * GB + i * 2 + slot, slot)
                row_dots(r, NG)

            with dve.Fori(1, GB // 2) as i:
                st.loop(i - 1, 2)
                hot_pair(i, 0, i)
            st.end(GB // 2 - 1)
            with dve.Fori(GB // 2, TB // 2) as r:
                st.loop(r - GB // 2, 1)
                row_dots(r, NG)
            st.end(TB // 2 - GB // 2)
            per_block = 2 * (GB // 2) + (TB - GB) // 2
            with dve.Fori(1, ND) as b:
                with dve.Fori(0, GB // 2) as i:
                    st.loop(b * per_block + i * 2 - per_block, 1)
                    st.var, st.per = b * per_block + i * 2 - per_block, 1
                    hot_pair(b * (TB // 2) + i, b, i)
                    st.n = st.start
                with dve.Fori(GB // 2, TB // 2) as i:
                    st.var = b * per_block + i + (GB // 2 - per_block)
                    row_dots(b * (TB // 2) + i, NG)
                    st.n = st.start
            st.n, st.var = st.start + (ND - 1) * per_block, None
            with dve.Fori(ND * TB // 2, G_BODY) as r:
                st.loop(r - ND * TB // 2, 1)
                row_dots(r, NG)
            st.end(G_BODY - ND * TB // 2)
            row_dots(G_BODY, G_REST)
            dve.engine_nop().then_inc(dots_done, 1)

            def weigh(m, raw, use, first=False):
                dve.wait_ge(weighted_in[raw], use * 32 + 32)
                if not first:
                    dve.wait_ge(wt_low, m - 1)
                dve.tensor_tensor(weighted[:, raw % 2], acts_in[:, raw], routes_in[:, raw],
                                  ALU.mult).then_inc(wt_ready, 1)

            def weighted_low(m, slot):
                dve.wait_ge(wt_high, m + 1)
                dve.tensor_tensor(wt_lo[:, slot], weighted[:, slot], wt_hi[:, slot].bitcast(F32),
                                  ALU.subtract).then_inc(wt_low, 1)

            for slot in range(2):
                weigh(slot, slot, 0, first=True)
            coef = pairs[:, WT, ND]
            dve.wait_ge(dots_gelu, 1)
            st.do(dve.tensor_tensor(coef, coef, dots, ALU.mult))

            def add_row(i, slot):
                dve.wait_ge(g_loaded[slot], i * 16 + (G_BODY + 2) * 16)
                dve.wait_ge(g_free[1 - slot], i + (G_BODY + 2 + slot))
                dve.scalar_tensor_tensor(out=yacc, in0=gathered[slot], scalar=coef[:, bass.ds(i * 2 + slot, 1)],
                                         in1=yacc, op0=ALU.mult, op1=ALU.add).then_inc(g_free[slot], 1)

            with dve.Fori(0, TILES // RAW - 1) as four:
                for j in range(RAW):
                    weighted_low(four * RAW + j, j % 2)
                    weigh(four * RAW + (j + 2), (j + 2) % RAW, four + (j + 2) // RAW)
                    add_row(four * 2 + j // 2, j % 2)
            for j in range(RAW):
                m = TILES - RAW + j
                weighted_low(m, j % 2)
                if j < 2:
                    weigh(m + 2, j + 2, TILES // RAW - 1)
                add_row(m // 2, j % 2)
            dve.wait_ge(g_free[1], G_BODY + 2 + TILES // 2)

            dve.wait_ge(tile_used, 2 * TILES)
            for b in range(NB):
                for half in range(D // NC):
                    cols_h = slice(half * NC, (half + 1) * NC)
                    total = ps[:, b * D // NC + half] if b < ND else yacc[:, cols_h]
                    st.inc(dve.tensor_tensor(out_buf[:, b, cols_h], total, mod[:, GATE2, cols_h], ALU.mult))
            st.wait()
            for b in range(NB):
                dve.tensor_tensor(x1[:, b], x1[:, b], out_buf[:, b], ALU.add).then_inc(x1_ready, 1)
            token_variance(3)
            root_reciprocal(5, n_v[:, 0:NB], n_s[:, 0:NB], n_y[:, 0:NB], n_t[:, 0:NB])
            dve.wait_ge(row_in, 64)
            for b in range(NB):
                dve.scalar_tensor_tensor(out=out_buf[:, b], in0=x1[:, b], scalar=n_y[:, b:b + 1], in1=row,
                                         op0=ALU.mult, op1=ALU.mult).then_inc(out_ready, 1)


_INS = ["x", "c", "positions", "w_ada", "b_ada", "norm_mix_gain", "w_in", "ret_gn_gain", "w_dw", "b_dw",
        "conv_ln_gain", "conv_ln_bias", "w_pw2", "w_out", "norm_ffn_gain", "w_peer_q", "peer_subkeys1",
        "peer_subkeys2", "peer_u", "peer_v", "final_norm_gain"]


def kernel(**inputs):
    import concourse.bacc as bacc
    from concourse.bass_utils import run_bass_kernel_spmd

    nc = bacc.Bacc("TRN2", target_bir_lowering=False, num_devices=1)
    arrays = {name: np.ascontiguousarray(inputs[name]) for name in _INS}
    arrays["tables"] = shape_tables()
    u = np.asarray(inputs["peer_u"])[0]
    arrays["peer_uT"] = np.ascontiguousarray(u.reshape(u.shape[0] // P, P, u.shape[1] // P, P).transpose(0, 3, 2, 1))
    args = {name: nc.dram_tensor(f"in_{name}", a.shape, mybir.dt.from_np(a.dtype), kind="ExternalInput").ap()
            for name, a in arrays.items()}
    out = nc.dram_tensor("out_block", arrays["x"].shape, F32, kind="ExternalOutput").ap()
    block_program(nc, **args, out=out)
    r = run_bass_kernel_spmd(nc, [{f"in_{name}": a for name, a in arrays.items()}], core_ids=[0])
    return r.results[0]["out_block"]
```
